# Optimizing a Trainium2 kernel written in Bass

```python
import math
import jax, jax.numpy as jnp
from jax import lax
import numpy as np

D_MODEL = 1024
BATCH = 1
SEQ = 1024
DEPTH = 1
DEC_BATCH = 8
DEC_SEQ = 8
PAST_LEN = 8192
PAGE_SIZE = 128

H_A = 4
DK_A = 128
DV_A = 256
W_A_QK = H_A * DK_A
W_A_V = H_A * DV_A
H_B = 8
DK_B = 128
DV_B = 128
W_B_QK = H_B * DK_B
W_B_V = H_B * DV_B
CONV_W = 4
C_CONV = 2 * W_B_QK + W_B_V
D_FF = 4 * D_MODEL
PLE_DIM = 256
MLSTM_CHUNK = 64
GDN_CHUNK = 64
EPS = 1e-6
F_BIAS_LO = 3.0
F_BIAS_HI = 6.0
IN_SIZES = (W_A_QK, W_A_QK, W_A_V, H_A, H_A, W_A_V, C_CONV, H_B, H_B, W_B_V, D_MODEL, D_MODEL)
N_IN = sum(IN_SIZES)

kernel_name = 'hybrid_mlstm_gdn_decode_step'

def _rmsnorm(x, g):
    xf = x.astype(jnp.float32)
    y = xf * lax.rsqrt(jnp.mean(xf * xf, axis=-1, keepdims=True) + EPS)
    return (y * g.astype(jnp.float32)).astype(x.dtype)

def _head_rms(t):
    return t * lax.rsqrt(jnp.mean(t * t, axis=-1, keepdims=True) + EPS)

def _l2norm(t):
    return t * lax.rsqrt(jnp.sum(t * t, axis=-1, keepdims=True) + EPS)

def _to_chunks(t, L):
    B, T, H = t.shape[:3]
    rest = t.shape[3:]
    t = t.reshape((B, T // L, L, H) + rest)
    return t.transpose((1, 0, 3, 2) + tuple(range(4, t.ndim)))

def _from_chunks(t):
    NC, B, H, L, E = t.shape
    return t.transpose(1, 0, 3, 2, 4).reshape(B, NC * L, H, E)

def _mlstm(q, k, v, i_pre, f_pre, C0, n0, m0):
    B, T, H, DK = q.shape
    L = math.gcd(T, MLSTM_CHUNK)
    q = q * (DK ** -0.5)
    qc, kc, vc = _to_chunks(q, L), _to_chunks(k, L), _to_chunks(v, L)
    ic = _to_chunks(i_pre, L)
    lfc = _to_chunks(jax.nn.log_sigmoid(f_pre), L)
    idx = jnp.arange(L)
    causal = idx[:, None] >= idx[None, :]

    def step(carry, inp):
        C, n, m = carry
        qx, kx, vx, ix, lfx = inp
        b = jnp.cumsum(lfx, axis=-1)
        dlog = jnp.where(causal, b[..., :, None] - b[..., None, :] + ix[..., None, :], -jnp.inf)
        inter = b + m[..., None]
        m_row = jnp.maximum(inter, jnp.max(dlog, axis=-1))
        dw = jnp.exp(dlog - m_row[..., None])
        w_inter = jnp.exp(inter - m_row)
        s = jnp.einsum('bhld,bhjd->bhlj', qx, kx) * dw
        num = w_inter[..., None] * jnp.einsum('bhld,bhde->bhle', qx, C) + jnp.einsum('bhlj,bhje->bhle', s, vx)
        nq = w_inter * jnp.einsum('bhld,bhd->bhl', qx, n) + jnp.sum(s, axis=-1)
        den = jnp.maximum(jnp.abs(nq), jnp.exp(-m_row))
        h = num / den[..., None]
        m_new = m_row[..., -1]
        dec = jnp.exp(b[..., -1] + m - m_new)
        wk = jnp.exp(ix + b[..., -1:] - b - m_new[..., None])
        C_new = dec[..., None, None] * C + jnp.einsum('bhl,bhld,bhle->bhde', wk, kx, vx)
        n_new = dec[..., None] * n + jnp.einsum('bhl,bhld->bhd', wk, kx)
        return (C_new, n_new, m_new), h

    (C, n, m), h = lax.scan(step, (C0, n0, m0), (qc, kc, vc, ic, lfc))
    return _from_chunks(h), C, n, m

def _gated_delta(q, k, v, g, beta, S0):
    B, T, H, DK = q.shape
    DV = v.shape[-1]
    L = math.gcd(T, GDN_CHUNK)
    q = q * (DK ** -0.5)
    qc, kc, vc = _to_chunks(q, L), _to_chunks(k, L), _to_chunks(v, L)
    gc, bc = _to_chunks(g, L), _to_chunks(beta, L)
    gam = jnp.cumsum(gc, axis=-1)
    idx = jnp.arange(L)
    lower = idx[:, None] >= idx[None, :]
    strict = idx[:, None] > idx[None, :]
    decay = jnp.exp(jnp.where(lower, gam[..., :, None] - gam[..., None, :], -jnp.inf))
    kb = kc * bc[..., None]
    m_kk = jnp.where(strict, jnp.einsum('nbhid,nbhjd->nbhij', kb, kc) * decay, 0.0)
    a_mat = m_kk + jnp.eye(L, dtype=m_kk.dtype)
    rhs = jnp.concatenate([vc * bc[..., None], kb * jnp.exp(gam)[..., None]], axis=-1)
    sol = lax.linalg.triangular_solve(a_mat, rhs, left_side=True, lower=True, unit_diagonal=True)
    w_v, w_k = sol[..., :DV], sol[..., DV:]
    qk = jnp.einsum('nbhid,nbhjd->nbhij', qc, kc) * decay
    q_dec = qc * jnp.exp(gam)[..., None]
    k_dec = kc * jnp.exp(gam[..., -1:] - gam)[..., None]
    g_last = jnp.exp(gam[..., -1])

    def step(S, inp):
        wv, wk, qkx, qd, kd, gl = inp
        u = wv - jnp.einsum('bhld,bhde->bhle', wk, S)
        o = jnp.einsum('bhld,bhde->bhle', qd, S) + jnp.einsum('bhlj,bhje->bhle', qkx, u)
        S = S * gl[..., None, None] + jnp.einsum('bhld,bhle->bhde', kd, u)
        return S, o

    S, o = lax.scan(step, S0, (w_v, w_k, qk, q_dec, k_dec, g_last))
    return _from_chunks(o), S

def _causal_conv(x, buf, w):
    T = x.shape[1]
    xp = jnp.concatenate([buf.astype(x.dtype), x], axis=1)
    out = xp[:, 0:T] * w[0]
    for j in range(1, CONV_W):
        out = out + xp[:, j:j + T] * w[j]
    return out, xp[:, -(CONV_W - 1):]

def _layer(x, p, C, n, m, S, conv_buf, g_mix, w_in, b_igate, b_fgate, g_norm_a, conv_w, a_log, dt_bias,
           g_norm_b, w_pa, w_pb, w_out, g_ffn, w_up, w_down, g_ple, w_pg, w_pp):
    f32 = jnp.float32
    B, T, _ = x.shape
    h = _rmsnorm(x, g_mix)
    proj = h @ w_in
    split_idx = np.cumsum(IN_SIZES)[:-1].tolist()
    (q_a, k_a, v_a, i_pre, f_pre, o_a, qkv_b, a_b, beta_b, z_b, gate_a, gate_b) = jnp.split(proj, split_idx, axis=-1)

    ha, C, n, m = _mlstm(q_a.reshape(B, T, H_A, DK_A).astype(f32), k_a.reshape(B, T, H_A, DK_A).astype(f32),
                         v_a.reshape(B, T, H_A, DV_A).astype(f32), i_pre.astype(f32) + b_igate.astype(f32),
                         f_pre.astype(f32) + b_fgate.astype(f32), C.astype(f32), n.astype(f32), m.astype(f32))
    ha = _head_rms(ha).reshape(B, T, W_A_V) * g_norm_a.astype(f32) * jax.nn.sigmoid(o_a.astype(f32))

    cv, conv_buf = _causal_conv(qkv_b, conv_buf, conv_w)
    cv = jax.nn.silu(cv.astype(f32))
    q_b = _l2norm(cv[..., :W_B_QK].reshape(B, T, H_B, DK_B))
    k_b = _l2norm(cv[..., W_B_QK:2 * W_B_QK].reshape(B, T, H_B, DK_B))
    v_b = cv[..., 2 * W_B_QK:].reshape(B, T, H_B, DV_B)
    g = -jnp.exp(a_log.astype(f32)) * jax.nn.softplus(a_b.astype(f32) + dt_bias.astype(f32))
    beta = jax.nn.sigmoid(beta_b.astype(f32))
    hb, S = _gated_delta(q_b, k_b, v_b, g, beta, S.astype(f32))
    hb = _head_rms(hb) * g_norm_b.astype(f32) * jax.nn.silu(z_b.astype(f32).reshape(B, T, H_B, DV_B))
    hb = hb.reshape(B, T, W_B_V)

    mix = jax.nn.sigmoid(gate_a) * (ha.astype(x.dtype) @ w_pa) + jax.nn.sigmoid(gate_b) * (hb.astype(x.dtype) @ w_pb)
    x = x + mix @ w_out
    u = _rmsnorm(x, g_ffn) @ w_up
    x = x + jnp.square(jax.nn.relu(u)) @ w_down
    x = x + jax.nn.sigmoid(_rmsnorm(x, g_ple) @ w_pg) * (p @ w_pp)
    return x, C, n, m, S, conv_buf

def setup_inputs(seed: int = 0) -> dict:
    key = jax.random.key(seed)
    ks = jax.random.split(key, 32)
    f32 = jnp.float32

    def nrm(k, shape, s):
        return (s * jax.random.normal(k, shape, dtype=f32)).astype(f32)

    dt = jnp.exp(jax.random.uniform(ks[16], (DEPTH, H_B), minval=math.log(1e-3), maxval=math.log(1e-1), dtype=f32))
    return {
        'x_prompt': nrm(ks[0], (BATCH, SEQ, D_MODEL), 1.0),
        'x_sample': nrm(ks[1], (DEC_BATCH, DEC_SEQ, D_MODEL), 1.0),
        'p_prompt': nrm(ks[2], (DEPTH, BATCH, SEQ, PLE_DIM), 1.0),
        'p_sample': nrm(ks[3], (DEPTH, DEC_BATCH, DEC_SEQ, PLE_DIM), 1.0),
        'state_mlstm_C': nrm(ks[4], (DEPTH, DEC_BATCH, H_A, DK_A, DV_A), 0.5),
        'state_mlstm_n': nrm(ks[5], (DEPTH, DEC_BATCH, H_A, DK_A), 0.5),
        'state_mlstm_m': 1.0 + nrm(ks[6], (DEPTH, DEC_BATCH, H_A), 0.5),
        'state_gdn_S': nrm(ks[7], (DEPTH, DEC_BATCH, H_B, DK_B, DV_B), 0.3),
        'state_gdn_conv': nrm(ks[8], (DEPTH, DEC_BATCH, CONV_W - 1, C_CONV), 1.0),
        'g_mix': 1.0 + nrm(ks[9], (DEPTH, D_MODEL), 0.05),
        'w_in': nrm(ks[10], (DEPTH, D_MODEL, N_IN), D_MODEL ** -0.5),
        'b_igate': nrm(ks[11], (DEPTH, H_A), 0.1),
        'b_fgate': jnp.linspace(F_BIAS_LO, F_BIAS_HI, H_A, dtype=f32)[None, :] + nrm(ks[12], (DEPTH, H_A), 0.1),
        'g_norm_a': 1.0 + nrm(ks[13], (DEPTH, W_A_V), 0.05),
        'conv_w': nrm(ks[14], (DEPTH, CONV_W, C_CONV), CONV_W ** -0.5),
        'a_log': jnp.log(jax.random.uniform(ks[15], (DEPTH, H_B), minval=1.0, maxval=16.0, dtype=f32)),
        'dt_bias': dt + jnp.log(-jnp.expm1(-dt)),
        'g_norm_b': 1.0 + nrm(ks[17], (DEPTH, DV_B), 0.05),
        'w_pa': nrm(ks[18], (DEPTH, W_A_V, D_MODEL), W_A_V ** -0.5),
        'w_pb': nrm(ks[19], (DEPTH, W_B_V, D_MODEL), W_B_V ** -0.5),
        'w_out': nrm(ks[20], (DEPTH, D_MODEL, D_MODEL), D_MODEL ** -0.5),
        'g_ffn': 1.0 + nrm(ks[21], (DEPTH, D_MODEL), 0.05),
        'w_up': nrm(ks[22], (DEPTH, D_MODEL, D_FF), D_MODEL ** -0.5),
        'w_down': nrm(ks[23], (DEPTH, D_FF, D_MODEL), D_FF ** -0.5),
        'g_ple': 1.0 + nrm(ks[24], (DEPTH, D_MODEL), 0.05),
        'w_pg': nrm(ks[25], (DEPTH, D_MODEL, D_MODEL), D_MODEL ** -0.5),
        'w_pp': nrm(ks[26], (DEPTH, PLE_DIM, D_MODEL), PLE_DIM ** -0.5),
        'g_final': 1.0 + nrm(ks[27], (D_MODEL,), 0.05),
    }

def reference(x_prompt, x_sample, p_prompt, p_sample, state_mlstm_C, state_mlstm_n, state_mlstm_m,
              state_gdn_S, state_gdn_conv, g_mix, w_in, b_igate, b_fgate, g_norm_a, conv_w, a_log, dt_bias,
              g_norm_b, w_pa, w_pb, w_out, g_ffn, w_up, w_down, g_ple, w_pg, w_pp, g_final):
    f32 = jnp.float32
    bp = x_prompt.shape[0]
    zC = jnp.zeros((bp, H_A, DK_A, DV_A), f32)
    zn = jnp.zeros((bp, H_A, DK_A), f32)
    zm = jnp.zeros((bp, H_A), f32)
    zS = jnp.zeros((bp, H_B, DK_B, DV_B), f32)
    zconv = jnp.zeros((bp, CONV_W - 1, C_CONV), x_prompt.dtype)
    xp, xs = x_prompt, x_sample
    pC, pn, pm, pS, pc = [], [], [], [], []
    sC, sn, sm, sS, sc = [], [], [], [], []
    for i in range(DEPTH):
        lw = (g_mix[i], w_in[i], b_igate[i], b_fgate[i], g_norm_a[i], conv_w[i], a_log[i], dt_bias[i],
              g_norm_b[i], w_pa[i], w_pb[i], w_out[i], g_ffn[i], w_up[i], w_down[i], g_ple[i], w_pg[i], w_pp[i])
        xp, c1, n1, m1, s1, v1 = _layer(xp, p_prompt[i], zC, zn, zm, zS, zconv, *lw)
        xs, c2, n2, m2, s2, v2 = _layer(xs, p_sample[i], state_mlstm_C[i], state_mlstm_n[i], state_mlstm_m[i],
                                        state_gdn_S[i], state_gdn_conv[i], *lw)
        pC.append(c1); pn.append(n1); pm.append(m1); pS.append(s1); pc.append(v1)
        sC.append(c2); sn.append(n2); sm.append(m2); sS.append(s2); sc.append(v2)
    y_prompt = _rmsnorm(xp, g_final)
    y_sample = _rmsnorm(xs, g_final)
    return (y_prompt, y_sample,
            jnp.stack(pC), jnp.stack(pn), jnp.stack(pm), jnp.stack(pS), jnp.stack(pc),
            jnp.stack(sC), jnp.stack(sn), jnp.stack(sm), jnp.stack(sS), jnp.stack(sc))


_drawn_inputs = setup_inputs


def setup_inputs(seed=0):
    import zlib

    import numpy as np

    out = dict(_drawn_inputs(seed))
    spreads = {}
    factors = {'g_norm_a': 3.872, 'g_norm_b': 3.759, 'g_ple': 30.338}
    for name, (base, spread) in spreads.items():
        noise = np.random.default_rng([zlib.crc32(name.encode()), seed]).standard_normal(out[name].shape)
        drawn = base * np.exp(spread * noise) if base else spread * noise
        out[name] = __import__('jax').numpy.asarray(drawn.astype(out[name].dtype))
    for name, factor in factors.items():
        out[name] = (out[name] * factor).astype(out[name].dtype)
    return out
```

```python
from contextlib import ExitStack
from math import log

import concourse.bass as bass
from concourse import mybir

F32 = mybir.dt.float32
F32R = mybir.dt.float32r
ALU = mybir.AluOpType
ACT = mybir.ActivationFunctionType
AX_X = mybir.AxisListType.X

P = 128
D = 1024
KT = D // P
SEQ = 1024
NB, NS = 8, 8
T = SEQ + NB * NS
L = 128
NC = SEQ // L
NCH = NC + 1
TP = NCH * L
GROUPS = [(0, 384), (384, 384), (768, T - 768)]
NG = len(GROUPS)
H_A, DK, DV_A = 4, 128, 256
H_B, DV_B = 8, 128
W = 4
HALO = W - 1
SP_LEN = NS + HALO
XP_LEN = HALO + SEQ + NB * SP_LEN
CV_LEN = XP_LEN - HALO
PLE = 256
F_FF = 4096
EPS = 1e-6
NEG = -1e30
LEVELS = 7

O_Q, O_K, O_V = 0, 512, 1024
O_I, O_F, O_O = 2048, 2052, 2056
O_QKV = 3080
O_A, O_BETA, O_Z = 6152, 6160, 6168
O_GA, O_GB = 7192, 8216


class Event:

    def __init__(self, sem, per=1):
        self.sem, self.per = sem, per

    def at(self, turn, n):
        return turn * self.per + n


class Landed(Event):

    def at(self, turn, n):
        return (turn * self.per + n) * 16


def wait(eng, ev, turn, n):
    eng.wait_ge(ev.sem, ev.at(turn, n))


class Chain:

    def __init__(self, eng, sem, per=0):
        self.eng, self.sem, self.per, self.turn, self.n = eng, sem, per, 0, 0

    def start(self, turn):
        self.turn, self.n = turn, 0

    def __call__(self, ins):
        self.n += 1
        ins.then_inc(self.sem, 1)
        self.eng.wait_ge(self.sem, self.turn * self.per + self.n)

    def end(self):
        assert self.n == self.per, (self.n, self.per)


class Banks:

    def __init__(self, tensors, slots, sem, name):
        self.tensors, self.slots = tensors, {s: i for i, s in enumerate(slots)}
        nb = len(tensors)
        self.uses = [len(range(b, len(slots), nb)) for b in range(nb)]
        self.full = [sem(f"{name}_full{b}") for b in range(nb)]
        self.took = [sem(f"{name}_taken{b}") for b in range(nb)]

    def _at(self, turn, slot):
        i = self.slots[slot]
        b = i % len(self.tensors)
        return b, turn * self.uses[b] + i // len(self.tensors)

    def tile(self, slot):
        return self.tensors[self.slots[slot] % len(self.tensors)]

    def claim(self, pe, turn, slot, *needs):
        b, n = self._at(0, slot)
        counts = {b: n}
        for need in needs:
            nb, m = self._at(0, need)
            counts[nb] = max(counts.get(nb, 0), m + 1)
        for nb, m in counts.items():
            m = turn * self.uses[nb] + m
            if not isinstance(m, int) or m > 0:
                pe.wait_ge(self.took[nb], m)
        return self.tensors[b]

    def filled(self, ins, slot):
        ins.then_inc(self.full[self.slots[slot] % len(self.tensors)], 1)

    def read(self, eng, turn, slot):
        b, n = self._at(turn, slot)
        eng.wait_ge(self.full[b], n + 1)
        return self.tensors[b]

    def taken(self, eng, turn, slot):
        b, n = self._at(turn, slot)
        eng.wait_ge(self.took[b], n + 1)

    def release(self, ins, slot):
        ins.then_inc(self.took[self.slots[slot] % len(self.tensors)], 1)


def chunks(ap):
    return ap.rearrange("p (c t) -> p c t", t=L)


def third(ap, t):
    return ap[:, 384 * t:384 * t + 384]


def three(ap):
    return ap.rearrange("p (c t) -> p c t", c=3)


def over_tokens(ap, n=L):
    return ap.unsqueeze(2).to_broadcast([ap.shape[0], ap.shape[1], n])


def over_chunks(ap, n=3):
    return ap.unsqueeze(1).to_broadcast([ap.shape[0], n, ap.shape[1]])


def slab_of(w, m, first=0, step=1):
    return w.rearrange("k (m s n) -> k m s n", s=step, n=P)[:, bass.ds(m, 1), first, :]


class Weights:

    def __init__(self, sb, sem, name, per, raw_slots=1):
        self.per = per
        self.rs = raw_slots
        self.raw = [sb(f"{name}_raw{s}", [P, KT, P], F32) for s in range(raw_slots)]
        self.hi = [sb(f"{name}_hi{s}", [P, KT, P], F32R) for s in range(2)]
        self.lo = [sb(f"{name}_lo{s}", [P, KT, P], F32R) for s in range(2)]
        self.landed = [sem(f"{name}_landed{s}") for s in range(raw_slots)]
        self.hi_done, self.lo_done = sem(f"{name}_hi_done"), sem(f"{name}_lo_done")

    def load(self, eng, h, j, src, kt=KT):
        n = h * self.per + j
        if not (isinstance(n, int) and n < self.rs):
            eng.wait_ge(self.lo_done, n - self.rs + 1)
        pattern = "(k p) a n -> p k (a n)" if len(src.shape) == 3 else "(k p) n -> p k n"
        eng.dma_start(self.raw[j % self.rs][:, 0:kt, :], src.rearrange(pattern, p=P)).then_inc(
            self.landed[j % self.rs], 16)

    def split_hi(self, dve, h, j, banks, kt=KT):
        n = h * self.per + j
        dve.wait_ge(self.landed[j % self.rs], (h * (self.per // self.rs) + j // self.rs + 1) * 16)
        if j >= 2:
            banks.read(dve, h, ("dense", j - 2, NG - 1))
        elif not (isinstance(n, int) and n < 2):
            banks.read(dve, h - 1, ("dense", j - 2 + self.per, NG - 1))
        dve.tensor_copy(self.hi[j % 2][:, 0:kt, :], self.raw[j % self.rs][:, 0:kt, :]).then_inc(self.hi_done, 1)

    def split_lo(self, pool, h, j, kt=KT):
        n = h * self.per + j
        pool.wait_ge(self.hi_done, n + 1)
        pool.tensor_tensor(self.lo[j % 2][:, 0:kt, :], self.raw[j % self.rs][:, 0:kt, :],
                           self.hi[j % 2][:, 0:kt, :], ALU.subtract).then_inc(self.lo_done, 1)

    def ready(self, pe, h, j):
        pe.wait_ge(self.lo_done, h * self.per + j + 1)

    def product(self, pe, j, out, hi, lo, kt=KT, start=True, stop=True):
        passes = [(self.lo[j % 2], hi), (self.hi[j % 2], lo), (self.hi[j % 2], hi)]
        for k in range(kt):
            for i, (a, b) in enumerate(passes):
                ins = pe.matmul(out, a[:, k, :], b[:, k, :], start=(start and k == 0 and i == 0),
                                stop=(stop and k == kt - 1 and i == 2))
        return ins


def build(nc, x_prompt, x_sample, p_prompt, p_sample, state_C, state_n, state_m, state_S, state_conv, g_mix, w_in,
          b_igate, b_fgate, g_norm_a, conv_w, a_log, dt_bias, g_norm_b, w_pa, w_pb, w_out, g_ffn, w_up, w_down,
          g_ple, w_pg, w_pp, g_final, y_prompt, y_sample, C_prompt, n_prompt, m_prompt, S_prompt, conv_prompt,
          C_sample, n_sample, m_sample, S_sample, conv_sample):
    ctx = ExitStack()

    sems = []

    def sem(name):
        sems.append(nc.alloc_semaphore(name=name))
        return sems[-1]

    def stage(body):
        body()
        nc.clear_and_free_semaphores(sems)
        nc.all_engine_barrier()
        sems.clear()

    def event(name, per=1):
        return Event(sem(name), per)

    def landed(name, per=1):
        return Landed(sem(name), per)

    def scratch(name, shape):
        return nc.dram_tensor(name, shape, F32, kind="Internal").ap()

    def sbuf_in(stack):
        return lambda name, shape, dt=F32: stack.enter_context(nc.sbuf_tensor(name, shape, dt))

    XT = scratch("XT", (KT, P, T))
    ROWS_A = scratch("ROWS_A", (H_A, 2, TP))
    DECS_A = scratch("DECS_A", (H_A, 16))
    ROWS_B = scratch("ROWS_B", (3, H_B, TP))
    HA = scratch("HA", (H_A, 2, P, T))
    HB = scratch("HB", (H_B, P, T))

    win = w_in[0]
    with ctx:
        ctx.enter_context(nc.allow_non_contiguous_dma(reason="small vectors, loaded once"))
        keep = sbuf_in(ctx)
        psum = [ctx.enter_context(nc.psum_tensor(f"bank{b}", [P, 512], F32)) for b in range(8)]
        ident = keep("ident", [P, P])
        ones = keep("ones", [P, P])
        eps = keep("eps", [P, 1])
        zero = keep("zero", [P, 1])
        lnq = keep("lnq", [P, 1])
        CO = keep("CO", [P, 3, H_B, 27])
        with ExitStack() as alias:
            hraw = sbuf_in(alias)("hraw", [P, 2 * KT * T])
        hs = ctx.enter_context(ExitStack())
        hbuf = sbuf_in(hs)
        hhi = hbuf("hhi", [P, KT, T], F32R)
        hlo = hbuf("hlo", [P, KT, T], F32R)
        gts = hs.enter_context(ExitStack())
        gbuf = sbuf_in(gts)
        GTB = gbuf("GTB", [P, H_B, 4, NCH])
        GTA = gbuf("GTA", [P, H_A, 3, NCH])
        CT = gbuf("CT", [P, 3, H_B, 28])
        madd = gbuf("madd", [P, P])
        madds = gbuf("madds", [P, P])
        ohb = gbuf("ohb", [P, NB])

        def prologue():
            with ExitStack() as st:
                sb = sbuf_in(st)
                xrow = sb("xrow", [P, NCH, D])
                xT = sb("xT", [P, KT, T])
                sq = sb("sq", [P, KT, 384])
                rb = sb("rb", [P, 384])
                hf = sb("hf", [P, KT, 384])
                gm = sb("gm", [P, KT])
                crow = sb("crow", [28, 3 * H_B * P])
                s_x = [sem(f"x_landed{i}") for i in range(3)]
                s_small = sem("small_landed")
                s_const = sem("const_ready")
                s_tr = [sem("x_turned_even"), sem("x_turned_odd")]
                s_cpy = [sem("x_copied_act"), sem("x_copied_dve")]
                s_sq, s_ss, s_ln = sem("x_squared"), sem("x_summed"), sem("x_rms")
                s_hf, s_hhi, s_hlo = sem("h_made"), sem("h_hi"), sem("h_lo")
                s_out = sem("xT_stored")
                s_ct, s_ctc = sem("conv_turned"), sem("conv_copied")
                with nc.Block() as block:
                    @block.sync
                    def _(sp):
                        xp = x_prompt[0].rearrange("(c p) d -> p c d", p=P)
                        for i in range(3):
                            n = 3 if i < 2 else 2
                            sp.dma_start(xrow[:, 3 * i:3 * i + n, :], xp[:, 3 * i:3 * i + n, :]).then_inc(s_x[i], 16)
                        sp.dma_start(xrow[0:NB * NS, NC, :], x_sample.rearrange("b t d -> (b t) d")).then_inc(s_x[2], 16)
                        sp.dma_start(gm[:], g_mix[0].rearrange("(k p) -> p k", p=P)).then_inc(s_small, 16)
                        sp.dma_start(crow[0:24, :], state_conv[0].rearrange("b j c -> (b j) c")).then_inc(s_small, 16)
                        sp.dma_start(crow[24:28, :], conv_w[0]).then_inc(s_small, 16)
                        sp.wait_ge(s_cpy[0], NCH)
                        sp.wait_ge(s_cpy[1], NCH)
                        sp.dma_start(XT.rearrange("k p t -> p k t"), xT[:]).then_inc(s_out, 16)
                        sp.wait_ge(s_out, 16)

                    @block.gpsimd
                    def _(pool):
                        pool.memset(ones[:], 1.0).then_inc(s_const, 1)
                        pool.memset(eps[:], EPS).then_inc(s_const, 1)
                        pool.memset(zero[:], 0.0).then_inc(s_const, 1)
                        pool.memset(lnq[:], -0.5 * log(DK)).then_inc(s_const, 1)
                        pool.memset(ident[:], 0.0).then_inc(s_const, 1)
                        pool.memset(madd[:], 0.0).then_inc(s_const, 1)
                        pool.wait_ge(s_const, 6)
                        pool.affine_select(out=ident[:], in_=ident[:], compare_op=ALU.not_equal, fill=1.0, base=0,
                                           pattern=[[-1, P]], channel_multiplier=1).then_inc(s_const, 1)
                        pool.affine_select(out=madd[:], in_=madd[:], compare_op=ALU.is_ge, fill=NEG, base=0,
                                           pattern=[[1, P]], channel_multiplier=-1).then_inc(s_const, 1)
                        pool.wait_ge(s_const, 8)
                        pool.affine_select(out=madds[:].rearrange("p (b t) -> p b t", t=NS),
                                           in_=madd[:].rearrange("p (b t) -> p b t", t=NS), compare_op=ALU.is_ge,
                                           fill=NEG, base=0, pattern=[[-NS, P // NS], [0, NS]],
                                           channel_multiplier=1).then_inc(s_const, 1)
                        pool.affine_select(out=ohb[:], in_=ones[:, 0:NB], compare_op=ALU.is_ge, fill=0.0, base=0,
                                           pattern=[[-NS, NB]], channel_multiplier=1).then_inc(s_const, 1)
                        pool.wait_ge(s_const, 10)
                        pool.affine_select(out=ohb[:], in_=ohb[:], compare_op=ALU.is_ge, fill=0.0, base=NS - 1,
                                           pattern=[[NS, NB]], channel_multiplier=-1).then_inc(s_const, 1)
                        for g, (a, w) in enumerate(GROUPS):
                            pool.wait_ge(s_hhi, g + 1)
                            pool.tensor_tensor(hlo[:, :, a:a + w], hf[:, :, 0:w], hhi[:, :, a:a + w],
                                               ALU.subtract).then_inc(s_hlo, 1)

                    def turned(eng, half, copy):
                        for c in range(NCH):
                            w = L if c < NC else NB * NS
                            eng.wait_ge(s_tr[half], c + 1)
                            src = psum[(2 * c + half) % 6][:].rearrange("p (k t) -> p k t", k=4)[:, :, 0:w]
                            copy(xT[:, 4 * half:4 * half + 4, c * L:c * L + w], src).then_inc(s_cpy[half], 1)
                            if c % 3 == 2:
                                yield c // 3

                    @block.tensor
                    def _(pe):
                        pe.wait_ge(s_const, 7)
                        for c in range(NCH):
                            w = L if c < NC else NB * NS
                            if c % 3 == 0:
                                pe.wait_ge(s_x[c // 3], 16 if c < 6 else 32)
                            for half in range(2):
                                if c >= 3:
                                    pe.wait_ge(s_cpy[half], c - 2)
                                for k in range(4):
                                    ins = pe.transpose(psum[(2 * c + half) % 6][:, k * P:k * P + w],
                                                       xrow[0:w, c, (4 * half + k) * P:(4 * half + k + 1) * P],
                                                       ident[0:w, 0:w])
                                ins.then_inc(s_tr[half], 1)
                            if c % 3 < 2:
                                continue
                            g = c // 3
                            w = GROUPS[g][1]
                            pe.wait_ge(s_sq, g + 1)
                            if g >= 2:
                                pe.wait_ge(s_ln, 2 * g - 3)
                            for k in range(KT):
                                ins = pe.matmul(psum[6 + g % 2][:, 0:w], ones[:], sq[:, k, 0:w], start=(k == 0),
                                                stop=(k == KT - 1))
                            ins.then_inc(s_ss, 1)
                        pe.wait_ge(s_small, 48)
                        pe.wait_ge(s_ln, 6)
                        for i in range(3 * H_B):
                            ins = pe.transpose(psum[6 + i // 12][:, 28 * (i % 12):28 * (i % 12) + 28],
                                               crow[:, P * i:P * i + P], ident[0:28, 0:28])
                            if i % 12 == 11:
                                ins.then_inc(s_ct, 1)

                    @block.scalar
                    def _(act):
                        act.wait_ge(s_const, 11)
                        for g in turned(act, 0, lambda o, i: act.activation(o, i, ACT.Copy)):
                            a, w = GROUPS[g]
                            act.wait_ge(s_cpy[0], 3 * g + 3)
                            act.wait_ge(s_cpy[1], 3 * g + 3)
                            if g:
                                act.wait_ge(s_ss, g)
                            act.activation(sq[:, :, 0:w], xT[:, :, a:a + w], ACT.Square).then_inc(s_sq, 1)
                            act.wait_ge(s_ss, g + 1)
                            if g:
                                act.wait_ge(s_hf, KT * g)
                            act.activation(rb[:, 0:w], psum[6 + g % 2][:, 0:w], ACT.Ln, scale=1.0 / D,
                                           bias=eps[:]).then_inc(s_ln, 1)
                            act.wait_ge(s_ln, 2 * g + 1)
                            act.activation(rb[:, 0:w], rb[:, 0:w], ACT.Exp, scale=-0.5).then_inc(s_ln, 1)

                    @block.vector
                    def _(dve):
                        dve.wait_ge(s_small, 48)
                        for g in turned(dve, 1, dve.tensor_copy):
                            a, w = GROUPS[g]
                            dve.wait_ge(s_ln, 2 * g + 2)
                            dve.wait_ge(s_cpy[1], 3 * g + 3)
                            if g:
                                dve.wait_ge(s_hlo, g)
                            for k in range(KT):
                                dve.scalar_tensor_tensor(hf[:, k, 0:w], xT[:, k, a:a + w], gm[:, k:k + 1],
                                                         rb[:, 0:w], ALU.mult, ALU.mult).then_inc(s_hf, 1)
                            dve.wait_ge(s_hf, KT * (g + 1))
                            dve.tensor_copy(hhi[:, :, a:a + w], hf[:, :, 0:w]).then_inc(s_hhi, 1)
                        for i in range(2):
                            dve.wait_ge(s_ct, i + 1)
                            src = psum[6 + i][:, 0:336].rearrange("p (m r) -> p m r", r=28)
                            dve.tensor_copy(CT[:].rearrange("p a b r -> p (a b) r")[:, 12 * i:12 * i + 12, :],
                                            src).then_inc(s_ctc, 1)

        def gates():
            RI, RF, RA, RB = 0, 32, 64, 96
            with ExitStack() as st:
                sb = sbuf_in(st)
                raw = sb("gw_raw", [P, KT, P])
                ghi = sb("gw_hi", [P, KT, P], F32R)
                glo = sb("gw_lo", [P, KT, P], F32R)
                bias = sb("g_bias", [P, 1])
                sign = sb("g_sign", [P, 1])
                coef = sb("g_coef", [P, 1])
                Y = sb("g_y", [P, T])
                A = sb("g_abs", [P, T])
                SPL = sb("g_softplus", [P, T])
                G = sb("g_log", [P, T])
                rmask = sb("g_reset", [P, T])
                CUM = sb("g_cum", [P, T])
                IR = sb("g_i", [P, T])
                ML = SEQ + 1 + NB * (NS + 1)
                LFP = sb("g_lfp", [P, ML])
                IP = sb("g_ip", [P, ML])
                MP = sb("g_mp", [P, ML])
                M = sb("g_m", [P, T])
                MPREV = sb("g_mprev", [P, 16])
                MLAST = sb("g_mlast", [P, 16])
                CLAST = sb("g_clast", [P, 16])
                CD = sb("g_cd", [P, 16])
                DEC = sb("g_dec", [P, 16])
                R = [sb(f"g_r{i}", [P, TP]) for i in range(4)]
                TT = sb("g_turned", [P, NCH, 3, P])
                s_z, s_w, s_b, s_p = sem("gate_zeroed"), sem("gate_w_landed"), sem("gate_b_landed"), sem("gate_product")
                s_hi, s_lo, s_y, s_i = sem("gate_w_hi"), sem("gate_w_lo"), sem("gate_y"), sem("gate_i_moved")
                s_m0, s_dve, s_act = sem("gate_m0_landed"), sem("gate_dve"), sem("gate_act")
                s_cum, s_m, s_exp = sem("gate_cumulated"), sem("gate_m"), sem("gate_exps")
                s_e, s_rows, s_t, s_tc = sem("gate_exponents"), sem("gate_stored"), sem("gate_turned"), sem("gate_copied")
                s_zw = sem("gate_w_zeroed")
                s_c, s_coef = sem("gate_consts"), sem("gate_coef")

                def prompt(x, r, c=L):
                    return x[r:r + 32, 0:SEQ].rearrange("p (c t) -> p c t", t=c)

                def sample(x, r):
                    return x[r:r + 32, SEQ:T].rearrange("p (b t) -> p b t", t=NS)

                def prompt_all(x):
                    return x[:, 0:SEQ].rearrange("p (c t) -> p c t", t=L)

                def sample_all(x):
                    return x[:, SEQ:T].rearrange("p (b t) -> p b t", t=NS)

                with nc.Block() as block:
                    @block.sync
                    def _(sp):
                        sp.wait_ge(s_zw, 1)
                        for o, n, r in ((O_I, H_A, RI), (O_F, H_A, RF), (O_A, H_B, RA), (O_BETA, H_B, RB)):
                            sp.dma_start(raw[:, :, r:r + n], win[:, o:o + n].rearrange("(k p) n -> p k n", p=P)).then_inc(s_w, 16)
                        sp.wait_ge(s_z, 4)
                        for v, n, r in ((b_igate, H_A, RI), (b_fgate, H_A, RF), (dt_bias, H_B, RA)):
                            sp.dma_start(bias[r:r + n, :], v.rearrange("a n -> n a")).then_inc(s_b, 16)
                        sp.dma_start(coef[RA:RA + H_B, :], a_log.rearrange("a n -> n a")).then_inc(s_b, 16)
                        m0 = IP[RF:RF + H_A, SEQ + 1:ML].rearrange("p (b t) -> p b t", t=NS + 1)
                        sp.dma_start(m0[:, :, 0], state_m[0].rearrange("b h -> h b")).then_inc(s_m0, 16)
                        sp.wait_ge(s_y, NG)
                        sp.dma_start(IR[RF:RF + H_A, :], Y[RI:RI + H_A, :]).then_inc(s_i, 16)
                        sp.wait_ge(s_m, 5)
                        sp.dma_start(m_prompt.rearrange("a b h -> h (a b)"), MLAST[RF:RF + H_A, NC - 1:NC]).then_inc(s_rows, 16)
                        sp.dma_start(m_sample[0].rearrange("b h -> h b"), MLAST[RF:RF + H_A, NC:16]).then_inc(s_rows, 16)
                        sp.wait_ge(s_exp, 9)
                        sp.wait_ge(s_e, 8)
                        sp.dma_start(ROWS_A[:, 0, :], R[3][RF:RF + H_A, :]).then_inc(s_rows, 16)
                        sp.dma_start(ROWS_B[0], R[3][RA:RA + H_B, :]).then_inc(s_rows, 16)
                        sp.dma_start(ROWS_A[:, 1, :], R[3][RB:RB + H_A, :]).then_inc(s_rows, 16)
                        sp.dma_start(ROWS_B[1], R[2][RA:RA + H_B, :]).then_inc(s_rows, 16)
                        sp.dma_start(ROWS_B[2], R[0][RB:RB + H_B, :]).then_inc(s_rows, 16)
                        sp.dma_start(DECS_A, DEC[RF:RF + H_A, :]).then_inc(s_rows, 16)
                        sp.wait_ge(s_rows, 8 * 16)

                    @block.gpsimd
                    def _(pool):
                        pool.memset(bias[:], 0.0).then_inc(s_z, 1)
                        pool.memset(coef[:], 0.0).then_inc(s_z, 1)
                        pool.memset(IP[:], 0.0).then_inc(s_z, 1)
                        pool.memset(IR[:], 0.0).then_inc(s_z, 1)
                        for r in R:
                            pool.memset(r[:], 0.0).then_inc(s_c, 1)
                        for i, (r, v) in enumerate(((RI, 1.0), (RF, -1.0), (RA, 1.0), (RB, -1.0))):
                            pool.wait_ge(s_c, 4 + i)
                            pool.memset(sign[r:r + 32, :], v).then_inc(s_c, 1)
                        pool.wait_ge(s_c, 8)
                        pool.memset(rmask[:], 1.0).then_inc(s_c, 1)
                        pool.memset(LFP[:], 0.0).then_inc(s_c, 1)
                        pool.wait_ge(s_c, 10)
                        pool.memset(prompt_all(rmask)[:, :, 0], 0.0).then_inc(s_c, 1)
                        pool.memset(sample_all(rmask)[:, :, 0], 0.0).then_inc(s_c, 1)
                        pool.memset(LFP[:, 0:1], NEG).then_inc(s_c, 1)
                        pool.memset(LFP[:, SEQ + 1:ML].rearrange("p (b t) -> p b t", t=NS + 1)[:, :, 0], NEG).then_inc(s_c, 1)

                    @block.tensor
                    def _(pe):
                        pe.wait_ge(s_lo, 1)
                        for g, (a, w) in enumerate(GROUPS):
                            for k in range(KT):
                                for i, (x, y) in enumerate(((glo, hhi), (ghi, hlo), (ghi, hhi))):
                                    ins = pe.matmul(psum[g][:, 0:w], x[:, k, :], y[:, k, a:a + w],
                                                    start=(k == 0 and i == 0), stop=(k == KT - 1 and i == 2))
                            ins.then_inc(s_p, 1)
                        pe.wait_ge(s_exp, 9)
                        pe.wait_ge(s_e, 8)
                        for c in range(NCH):
                            if c >= 2:
                                pe.wait_ge(s_tc, c - 1)
                            for i in range(3):
                                ins = pe.transpose(psum[4 + c % 2][:, i * P:i * P + P], R[i][:, c * L:c * L + L], ident[:])
                            ins.then_inc(s_t, 1)

                    @block.scalar
                    def _(act):
                        act.wait_ge(s_b, 64)
                        act.activation(coef[RA:RA + 32, :], coef[RA:RA + 32, :], ACT.Exp).then_inc(s_coef, 1)
                        act.wait_ge(s_y, NG)
                        act.activation(A[:], Y[:], ACT.Abs).then_inc(s_act, 1)
                        act.wait_ge(s_act, 1)
                        act.activation(A[:], A[:], ACT.Exp, scale=-1.0).then_inc(s_act, 1)
                        act.wait_ge(s_act, 2)
                        act.activation(A[:], A[:], ACT.Ln, bias=ones[:, 0:1]).then_inc(s_act, 1)
                        act.wait_ge(s_dve, 3)
                        act.wait_ge(s_c, 4)
                        act.activation(R[0][RB:P, 0:T], G[RB:P, :], ACT.Exp).then_inc(s_exp, 1)
                        act.wait_ge(s_cum, 1)
                        act.activation(R[2][RA:RA + 32, 0:T], CUM[RA:RA + 32, :], ACT.Exp).then_inc(s_exp, 1)
                        act.wait_ge(s_m, 2)
                        act.activation(R[2][RF:RF + 32, 0:T], M[RF:RF + 32, :], ACT.Exp, scale=-1.0).then_inc(s_exp, 1)
                        act.wait_ge(s_e, 3)
                        act.activation(DEC[RF:RF + 32, :], DEC[RF:RF + 32, :], ACT.Exp).then_inc(s_exp, 1)
                        act.wait_ge(s_e, 5)
                        act.activation(R[1][RF:RF + 32, 0:T], R[1][RF:RF + 32, 0:T], ACT.Exp).then_inc(s_exp, 1)
                        act.wait_ge(s_e, 6)
                        act.activation(R[1][RA:RA + 32, 0:T], R[1][RA:RA + 32, 0:T], ACT.Exp).then_inc(s_exp, 1)
                        act.wait_ge(s_e, 7)
                        act.activation(R[3][RB:RB + 32, 0:T], MP[RF:RF + 32, 0:T], ACT.Exp).then_inc(s_exp, 3)
                        for c in range(NCH):
                            act.wait_ge(s_t, c + 1)
                            act.activation(TT[:, c], psum[4 + c % 2][:, 0:3 * P].rearrange("p (i r) -> p i r", i=3),
                                           ACT.Copy).then_inc(s_tc, 1)

                    @block.vector
                    def _(dve):
                        ch = Chain(dve, s_dve)
                        dve.memset(raw[:], 0.0).then_inc(s_zw, 1)
                        dve.wait_ge(s_w, 64)
                        dve.tensor_copy(ghi[:], raw[:]).then_inc(s_hi, 1)
                        dve.wait_ge(s_hi, 1)
                        dve.tensor_tensor(glo[:], raw[:], ghi[:], ALU.subtract).then_inc(s_lo, 1)
                        dve.wait_ge(s_b, 64)
                        dve.wait_ge(s_c, 8)
                        for g, (a, w) in enumerate(GROUPS):
                            dve.wait_ge(s_p, g + 1)
                            dve.tensor_scalar(Y[:, a:a + w], psum[g][:, 0:w], bias[:], sign[:], ALU.add, ALU.mult).then_inc(s_y, 1)
                        dve.wait_ge(s_coef, 1)
                        ch(dve.memset(coef[RF:RF + 32, :], 1.0))
                        dve.wait_ge(s_act, 3)
                        dve.wait_ge(s_y, NG)
                        ch(dve.scalar_tensor_tensor(SPL[:], Y[:], 0.0, A[:], ALU.max, ALU.add))
                        dve.tensor_scalar(G[0:RB, :], SPL[0:RB, :], coef[0:RB, :], -1.0, ALU.mult, ALU.mult)
                        ch(dve.tensor_scalar(G[RB:P, :], SPL[RB:P, :], -1.0, None, ALU.mult))
                        dve.wait_ge(s_c, 14)
                        dve.memset(R[2][RF:RF + 32, T:TP], 1.0)
                        dve.tensor_tensor_scan(CUM[:], rmask[:], G[:], 0.0, ALU.mult, ALU.add).then_inc(s_cum, 1)
                        f = slice(RF, RF + 32)
                        a = slice(RA, RA + 32)
                        dve.wait_ge(s_i, 16)
                        dve.wait_ge(s_m0, 16)
                        lp = LFP[f, SEQ + 1:ML].rearrange("p (b t) -> p b t", t=NS + 1)
                        ip = IP[f, SEQ + 1:ML].rearrange("p (b t) -> p b t", t=NS + 1)
                        mp = MP[f, SEQ + 1:ML].rearrange("p (b t) -> p b t", t=NS + 1)
                        dve.tensor_copy(LFP[f, 1:SEQ + 1], G[f, 0:SEQ])
                        dve.tensor_copy(lp[:, :, 1:], sample(G, RF))
                        dve.tensor_copy(IP[f, 1:SEQ + 1], IR[f, 0:SEQ])
                        ch(dve.tensor_copy(ip[:, :, 1:], sample(IR, RF)))
                        ch(dve.tensor_tensor_scan(MP[f, :], LFP[f, :], IP[f, :], 0.0, ALU.add, ALU.max))
                        dve.tensor_copy(M[f, 0:SEQ], MP[f, 1:SEQ + 1]).then_inc(s_m, 1)
                        dve.tensor_copy(sample(M, RF), mp[:, :, 1:]).then_inc(s_m, 1)
                        mpc = MP[f, 0:SEQ].rearrange("p (c t) -> p c t", t=L)
                        dve.tensor_copy(MPREV[f, 0:NC], mpc[:, :, 0])
                        dve.tensor_copy(MPREV[f, NC:16], mp[:, :, 0])
                        dve.wait_ge(s_m, 2)
                        dve.tensor_copy(MLAST[f, 0:NC], prompt(M, RF)[:, :, L - 1]).then_inc(s_m, 1)
                        dve.tensor_copy(MLAST[f, NC:16], sample(M, RF)[:, :, NS - 1]).then_inc(s_m, 1)
                        dve.wait_ge(s_cum, 1)
                        for r in (RF, RA):
                            dve.tensor_copy(CLAST[r:r + 32, 0:NC], prompt(CUM, r)[:, :, L - 1])
                            ins = dve.tensor_copy(CLAST[r:r + 32, NC:16], sample(CUM, r)[:, :, NS - 1])
                        ins.then_inc(s_m, 1)
                        dve.wait_ge(s_m, 5)
                        dve.tensor_tensor(R[3][f, 0:T], CUM[f, :], M[f, :], ALU.subtract).then_inc(s_e, 1)
                        dve.tensor_tensor(R[0][f, 0:T], IR[f, :], CUM[f, :], ALU.subtract).then_inc(s_e, 1)
                        ch(dve.tensor_tensor(CD[f, :], CLAST[f, :], MLAST[f, :], ALU.subtract))
                        dve.tensor_tensor(DEC[f, :], CD[f, :], MPREV[f, :], ALU.add).then_inc(s_e, 1)
                        dve.wait_ge(s_e, 2)
                        for part, lo, hi, n in ((prompt, 0, NC, L), (sample, NC, 16, NS)):
                            dve.tensor_tensor(part(R[1], RF), part(R[0], RF), over_tokens(CD[f, lo:hi], n), ALU.add).then_inc(s_e, 1)
                        dve.tensor_tensor(prompt(R[1], RA), over_tokens(CLAST[a, 0:NC], L), prompt(CUM, RA), ALU.subtract)
                        dve.tensor_tensor(sample(R[1], RA), over_tokens(CLAST[a, NC:16], NS), sample(CUM, RA),
                                          ALU.subtract).then_inc(s_e, 1)
                        dve.wait_ge(s_m, 5)
                        dve.tensor_tensor(prompt(MP, RF), prompt(R[3], RF), over_tokens(MPREV[f, 0:NC], L), ALU.add)
                        dve.tensor_tensor(sample(MP, RF), sample(R[3], RF), over_tokens(MPREV[f, NC:16], NS), ALU.add).then_inc(s_e, 1)
                        dve.tensor_copy(R[3][a, 0:T], CUM[a, :])
                        dve.tensor_scalar(R[0][a, 0:T], CUM[a, :], -1.0, None, ALU.mult).then_inc(s_e, 1)
                        dve.wait_ge(s_tc, NCH)
                        for h0, i, r in ((0, 0, RA), (1, 1, RA), (2, 0, RB), (3, 2, RA)):
                            ins = dve.tensor_copy(GTB[:, :, h0, :].rearrange("p h c -> p c h"), TT[:, :, i, r:r + H_B])
                        ch(ins)
                        dve.tensor_tensor(GTB[:, :, 3, :], GTB[:, :, 3, :], GTB[:, :, 2, :], ALU.mult)
                        for v, i in ((0, 0), (1, 1), (2, 2)):
                            dve.tensor_copy(GTA[:, :, v, :].rearrange("p h c -> p c h"), TT[:, :, i, RF:RF + H_A])

        def delta():
            OFFS = (O_QKV + H_B * DK, O_QKV, O_QKV + 2 * H_B * DK, O_Z)
            TAP = (1, 0, 2)
            dense = [("dense", j, g) for j in range(4) for g in range(NG)]
            inv = [(n, t) for t in range(3) for n in ("kt", "vt", "p1", "p2")] + [("at", t) for t in range(3)]
            for l in range(1, LEVELS):
                inv += [("z", l, t) for t in range(3)]
                for t in range(3):
                    inv += ([("d", l, t)] if l < LEVELS - 1 else []) + [("e", l, t)]
            inv += [("wk", t) for t in range(3)]
            norms = [("n", j, g) for j in range(2) for g in range(NG)]
            main = dense[:9] + norms + dense[9:] + inv
            scan = [(n, c) for c in range(NCH) for n in (("u", "s", "o") if c < NC else ("u", "o", "s0", "s1"))] + \
                   [("turn", t) for t in range(3)]
            B = Banks(psum[0:6], main, sem, "b_main")
            SB = Banks(psum[6:8], scan, sem, "b_scan")
            with ExitStack() as st:
                sb = sbuf_in(st)
                WS = Weights(sb, sem, "b_w", per=4)
                XPB = sb("b_xp", [P, XP_LEN])
                CV = sb("b_cv", [P, XP_LEN])
                KN, QN, VS = (sb(n, [P, TP]) for n in ("b_k", "b_q", "b_v"))
                ZS = sb("b_z", [P, T])
                GAM, EG, KB = (sb(n, [P, TP]) for n in ("b_gam", "b_eg", "b_kb"))
                DT, QKT, AT, DM, E = (sb(n, [P, TP]) for n in ("b_dt", "b_qkt", "b_at", "b_d", "b_e"))
                Z = DT
                SQ = (DT, AT)
                KD, KBE, BV, WKT, QD = (sb(n, [P, TP]) for n in ("b_kd", "b_kbe", "b_bv", "b_wkt", "b_qd"))
                O = KBE
                UM = DM
                TAPS = sb("b_taps", [P, 3, 28])
                HG = sb("b_hg", [P, 4, NCH])
                GL = sb("b_gl", [P, 16])
                SM = sb("b_sm", [P, LEVELS, P])
                off = sb("b_off", [P, P])
                SMT = sb("b_smt", [P, P])
                S = [sb(f"b_s{i}", [P, P]) for i in range(2)]
                U = [sb(f"b_u{i}", [P, P]) for i in range(2)]
                SS = sb("b_ss", [P, NB, P])
                WKM, QDM = sb("b_wkm", [P, NB * (P + NS)]), sb("b_qdm", [P, NB * (P + NS)])
                gb, gbh = sb("b_gb", [P, 1]), sb("b_gbh", [P, 1])
                ssum, rr = sb("b_ssum", [P, NCH]), sb("b_rr", [P, NCH])

                MASKS = 7 + 4 * LEVELS + 2
                s_mask, s_gb = sem("b_masks"), sem("b_gb_landed")
                s_row = [landed(f"b_row{i}_landed") for i in range(3)]
                s_ss = landed("b_ss_landed")
                s_st = landed("b_state_stored", 2)
                s_hb = landed("b_out_stored")
                taps = event("b_taps_ready")
                halos = event("b_halo_ready", 3)
                tap0 = event("b_tap0", 3)
                CONV = 3 * 3
                cv = event("b_conv_step", CONV)
                silus = event("b_silu", 3)
                sq = event("b_squares", 2)
                rn = event("b_norms", 2)
                kn = event("b_unit", 2)
                kb, qd = event("b_kb_ready"), event("b_qd_ready")
                gl = event("b_gl_ready")
                dx, dt = event("b_exponents", 3), event("b_decays", 3)
                diag, e0 = event("b_at_diagonal", 6), event("b_e0", 3)
                masked = event("b_masked_ready")
                um, sgl = event("b_um_ready"), event("b_ss_decayed")
                osum, half = event("b_o_sums", 2), event("b_gb_halved")
                onorm, oscaled = event("b_o_norms", 2), event("b_o_scaled")
                HBT = KD
                SQO = BV

                def parts(l, t):
                    return 2 if t == 2 and (1 << l) >= NS else 3

                def sequences(ap):
                    return ap[:, SEQ:T].rearrange("p (b t) -> p b t", t=NS)

                def blocks(ap):
                    return ap[:].rearrange("p (b x) -> p b x", x=P + NS)[:, :, 0:NS]

                with nc.Block() as block:
                    @block.sync
                    def _(sp):
                        def slab(h, j):
                            WS.load(sp, h, j, win[:, bass.ds(h * P + OFFS[j], P)])

                        def turn(h, scan, nxt):
                            if scan:
                                wait(sp, qd, h - 1, 1)
                                wait(sp, gl, h - 1, 1)
                                B.taken(sp, h - 1, ("wk", 2))
                            for i, dst in enumerate((GAM, EG, KB)):
                                sp.dma_start(dst[:], ROWS_B[i, bass.ds(h, 1), :].to_broadcast([P, TP])).then_inc(s_row[i].sem, 16)
                            for j in (1, 2, 3):
                                slab(h, j)
                            if nxt:
                                slab(h + 1, 0)
                            if scan:
                                stores(h - 1)
                            sp.dma_start(SS[:], state_S[0, :, bass.ds(h, 1)].rearrange("b a k v -> k (b a) v")).then_inc(s_ss.sem, 16)

                        def stores(h):
                            SB.taken(sp, h, ("s", NC - 1))
                            sp.dma_start(S_prompt[0, 0, bass.ds(h, 1)].rearrange("a k v -> k (a v)"), S[NC % 2][:]).then_inc(s_st.sem, 16)
                            SB.taken(sp, h, ("s1", NC))
                            sp.dma_start(S_sample[0, :, bass.ds(h, 1)].rearrange("b a k v -> k (b a) v"), SS[:]).then_inc(s_st.sem, 16)
                            SB.taken(sp, h, ("turn", 2))
                            sp.dma_start(HB[bass.ds(h, 1)].rearrange("a p t -> p (a t)"), HBT[:, 0:T]).then_inc(s_hb.sem, 16)
                            wait(sp, s_st, h, 2)

                        slab(0, 0)
                        sp.dma_start(gb[:], g_norm_b.rearrange("a n -> n a")).then_inc(s_gb, 16)
                        turn(0, False, True)
                        with sp.Fori(1, H_B - 1) as h:
                            turn(h, True, True)
                        turn(H_B - 1, True, False)
                        stores(H_B - 1)
                        wait(sp, s_hb, H_B - 1, 1)

                    @block.gpsimd
                    def _(pool):
                        WS.split_lo(pool, 0, 0)
                        for x in (KN, QN, VS):
                            pool.memset(x[:, T:TP], 0.0).then_inc(s_mask, 1)
                        pool.memset(WKM[:], 0.0).then_inc(s_mask, 1)
                        pool.memset(QDM[:], 0.0).then_inc(s_mask, 1)
                        for l in range(LEVELS):
                            s = 1 << l
                            pool.memset(SM[:, l, :], 0.0).then_inc(s_mask, 1)
                        pool.memset(SMT[:], 0.0).then_inc(s_mask, 1)
                        pool.affine_select(out=off[:], in_=ones[:], compare_op=ALU.not_equal, fill=0.0, base=0,
                                           pattern=[[-1, P]], channel_multiplier=1).then_inc(s_mask, 1)
                        n = 7 + LEVELS
                        pool.wait_ge(s_mask, n)
                        for l in range(LEVELS):
                            s = 1 << l
                            v = SM[:, l, :].rearrange("p (m two s) -> p m two s", two=2, s=s)[:, :, 0, :]
                            pool.affine_select(out=v, in_=v, compare_op=ALU.is_gt, fill=-1.0, base=s,
                                               pattern=[[2 * s, P // (2 * s)], [0, s]], channel_multiplier=-1).then_inc(s_mask, 1)
                            n += 1
                            pool.wait_ge(s_mask, n)
                            pool.affine_select(out=v, in_=v, compare_op=ALU.is_gt, fill=0.0, base=2 * s,
                                               pattern=[[2 * s, P // (2 * s)], [0, s]], channel_multiplier=-1).then_inc(s_mask, 1)
                            n += 1
                            pool.wait_ge(s_mask, n)
                            pool.affine_select(out=SM[:, l, :], in_=SM[:, l, :], compare_op=ALU.not_equal, fill=1.0, base=0,
                                               pattern=[[-1, P]], channel_multiplier=1).then_inc(s_mask, 1)
                            n += 1
                        v = SMT[:].rearrange("p (m two) -> p m two", two=2)[:, :, 1]
                        pool.affine_select(out=v, in_=v, compare_op=ALU.not_equal, fill=-1.0, base=0,
                                           pattern=[[2, P // 2]], channel_multiplier=-1).then_inc(s_mask, 1)
                        pool.wait_ge(s_mask, n + 1)
                        pool.affine_select(out=SMT[:], in_=SMT[:], compare_op=ALU.not_equal, fill=1.0, base=0,
                                           pattern=[[-1, P]], channel_multiplier=1).then_inc(s_mask, 1)

                        def turn(h, scan, nxt):
                            for j in (1, 2, 3):
                                WS.split_lo(pool, h, j)
                            if nxt:
                                WS.split_lo(pool, h + 1, 0)
                            wait(pool, kn, h, 1)
                            wait(pool, s_row[2], h, 1)
                            pool.tensor_tensor(KB[:], KN[:], KB[:], ALU.mult).then_inc(kb.sem, 1)
                            wait(pool, kn, h, 2)
                            wait(pool, s_row[1], h, 1)
                            if scan:
                                SB.taken(pool, h - 1, ("o", NC))
                            pool.tensor_tensor(QD[:], QN[:], EG[:], ALU.mult).then_inc(qd.sem, 1)
                            for t in range(3):
                                v = three(third(AT, t))
                                B.taken(pool, h, ("p1", t))
                                pool.tensor_tensor(v, v, over_chunks(off[:]), ALU.mult).then_inc(diag.sem, 1)
                                wait(pool, diag, h, 2 * t + 1)
                                pool.tensor_tensor(v, v, over_chunks(ident[:]), ALU.add).then_inc(diag.sem, 1)
                            for t in range(3):
                                wait(pool, diag, h, 2 * t + 2)
                                pool.tensor_tensor(three(third(E, t)), three(third(AT, t)), over_chunks(SMT[:]),
                                                   ALU.mult).then_inc(e0.sem, 1)

                        turn(0, False, True)
                        with pool.Fori(1, H_B - 1) as h:
                            turn(h, True, True)
                        turn(H_B - 1, True, False)

                    @block.tensor
                    def _(pe):
                        def group(h, j, g):
                            a, w = GROUPS[g]
                            slot = ("dense", j, g)
                            if g == 0:
                                WS.ready(pe, h, j)
                            bank = B.claim(pe, h, slot)
                            B.filled(WS.product(pe, j, bank[:, 0:w], hhi[:, :, a:a + w], hlo[:, :, a:a + w]), slot)

                        def norm(h, j, g):
                            a, w = GROUPS[g]
                            if g == 0:
                                wait(pe, sq, h, j + 1)
                            bank = B.claim(pe, h, ("n", j, g))
                            B.filled(pe.matmul(bank[:, 0:w], ones[:], SQ[j][:, a:a + w], start=True, stop=True), ("n", j, g))

                        def scan_chunk(h, c):
                            a = c * L
                            u = SB.claim(pe, h, ("u", c))[:, 0:P]
                            if c == NC:
                                wait(pe, s_ss, h, 1)
                                wait(pe, masked, h, 1)
                            ins = pe.matmul(u, E[:, a:a + L], BV[:, a:a + L], start=True, stop=(c == 0))
                            if 0 < c < NC:
                                SB.taken(pe, h, ("s", c - 1))
                                ins = pe.matmul(u, WKT[:, a:a + L], S[c % 2][:], start=False, stop=True)
                            if c == NC:
                                for b in range(NB):
                                    ins = pe.matmul(u, WKM[:, P * b:P * b + P], SS[:, b, :], start=False, stop=(b == NB - 1))
                            SB.filled(ins, ("u", c))
                            if c < NC:
                                s = SB.claim(pe, h, ("s", c), ("u", c))[:, 0:P]
                                SB.filled(pe.matmul(s, KD[:, a:a + L], U[c % 2][:], start=True, stop=True), ("s", c))
                            o = SB.claim(pe, h, ("o", c), ("u", c))[:, 0:P]
                            ins = pe.matmul(o, QKT[:, a:a + L], U[c % 2][:], start=True, stop=(c == 0))
                            if 0 < c < NC:
                                ins = pe.matmul(o, QD[:, a:a + L], S[c % 2][:], start=False, stop=True)
                            if c == NC:
                                for b in range(NB):
                                    ins = pe.matmul(o, QDM[:, P * b:P * b + P], SS[:, b, :], start=False, stop=(b == NB - 1))
                            SB.filled(ins, ("o", c))
                            if c == NC:
                                wait(pe, um, h, 1)
                                for i in range(2):
                                    s = SB.claim(pe, h, (f"s{i}", c))
                                    SB.filled(pe.matmul(s[:], KD[:, a:a + L], UM[:, 512 * i:512 * i + 512], start=True,
                                                        stop=True), (f"s{i}", c))

                        def scan_turn(h):
                            wait(pe, oscaled, h, 1)
                            for t in range(3):
                                bank = SB.claim(pe, h, ("turn", t))
                                for i in range(3):
                                    a = (3 * t + i) * L
                                    ins = pe.transpose(bank[:, i * L:i * L + L], O[:, a:a + L], ident[:])
                                SB.filled(ins, ("turn", t))

                        def of_chunks(h, slot, lhs, rhs, needs=(), transpose=False, n=3):
                            bank = B.claim(pe, h, slot, *needs)
                            t = slot[-1]
                            for i in range(n):
                                a = (3 * t + i) * L
                                out = bank[:, i * L:i * L + L]
                                if transpose:
                                    ins = pe.transpose(out, lhs[:, a:a + L], ident[:])
                                else:
                                    ins = pe.matmul(out, lhs[:, a:a + L], rhs[:, a:a + L], start=True, stop=True)
                            B.filled(ins, slot)

                        def inverse(h):
                            wait(pe, kn, h, 2)
                            wait(pe, kb, h, 1)
                            wait(pe, silus, h, 3)
                            for t in range(3):
                                of_chunks(h, ("kt", t), KN, None, transpose=True)
                                of_chunks(h, ("vt", t), VS, None, transpose=True)
                                of_chunks(h, ("p1", t), KN, KB)
                                of_chunks(h, ("p2", t), KN, QN)
                            for t in range(3):
                                wait(pe, diag, h, 2 * t + 2)
                                of_chunks(h, ("at", t), AT, None, transpose=True)
                            for l in range(1, LEVELS):
                                for t in range(3):
                                    if l == 1:
                                        wait(pe, e0, h, t + 1)
                                    of_chunks(h, ("z", l, t), AT, DM, [("at", t) if l == 1 else ("d", l - 1, t)], n=parts(l, t))
                                for t in range(3):
                                    needs = [("z", l, t)] + ([("e", l - 1, t)] if l > 1 else [])
                                    if l < LEVELS - 1:
                                        of_chunks(h, ("d", l, t), E, Z, needs, n=parts(l, t))
                                    of_chunks(h, ("e", l, t), Z, E, needs, n=parts(l, t))
                            for t in range(3):
                                of_chunks(h, ("wk", t), KBE, E, [("e", LEVELS - 1, t), ("kt", t)])

                        def turn(h, scan):
                            for i in range(12):
                                if i == 3 and not scan:
                                    pe.wait_ge(s_mask, MASKS)
                                group(h, i // 3, i % 3)
                                if i == 8:
                                    for j in range(2):
                                        for g in range(NG):
                                            norm(h, j, g)
                                if scan and i < NCH:
                                    scan_chunk(h - 1, i)
                            if scan:
                                scan_turn(h - 1)
                            inverse(h)

                        turn(0, False)
                        with pe.Fori(1, H_B) as h:
                            turn(h, True)
                        for c in range(NCH):
                            scan_chunk(H_B - 1, c)
                        scan_turn(H_B - 1)

                    @block.scalar
                    def _(act):
                        act.wait_ge(s_mask, MASKS)

                        def seq(x):
                            return x[:, HALO + SEQ:XP_LEN].rearrange("p (b t) -> p b t", t=SP_LEN)

                        def halo(h, j):
                            if j == 0:
                                wait(act, taps, h, 1)
                            else:
                                wait(act, cv, h, 3 * j)
                            act.activation(XPB[:, 0:HALO], ident[:, 0:HALO], ACT.Copy, scale=0.0)
                            act.activation(seq(XPB)[:, :, 0:HALO], TAPS[:, TAP[j], 0:24].rearrange("p (b t) -> p b t", t=HALO),
                                           ACT.Copy).then_inc(halos.sem, 1)

                        def copy_out(h, j, g):
                            a, w = GROUPS[g]
                            src = B.read(act, h, ("dense", j, g))
                            n = min(w, SEQ - a)
                            ins = act.activation(XPB[:, HALO + a:HALO + a + n], src[:, 0:n], ACT.Copy)
                            if n < w:
                                ins = act.activation(seq(XPB)[:, :, HALO:], src[:, n:w].rearrange("p (b t) -> p b t", t=NS), ACT.Copy)
                            B.release(ins, ("dense", j, g))

                        def first_tap(h, j):
                            wait(act, halos, h, j + 1)
                            B.taken(act, h, ("dense", j, NG - 1))
                            if j:
                                wait(act, silus, h, j)
                            act.activation(CV[:, 0:CV_LEN], XPB[:, 0:CV_LEN], ACT.Copy, scale=TAPS[:, TAP[j], 24:25]).then_inc(tap0.sem, 1)
                            act.activation(CO[:, TAP[j], bass.ds(h, 1), 0:HALO], XPB[:, SEQ:SEQ + HALO].unsqueeze(1), ACT.Copy)
                            act.activation(CO[:, TAP[j], bass.ds(h, 1), HALO:27].rearrange("p a (b t) -> p (a b) t", t=HALO),
                                           seq(XPB)[:, :, NS:SP_LEN], ACT.Copy)

                        def silu(h, j, dst):
                            wait(act, cv, h, 3 * j + 3)
                            act.activation(dst[:, 0:SEQ], CV[:, 0:SEQ], ACT.Silu)
                            act.activation(sequences(dst), seq(CV)[:, :, 0:NS], ACT.Silu).then_inc(silus.sem, 1)

                        def squares(h, j, src):
                            wait(act, silus, h, j + 1)
                            act.activation(SQ[j][:, 0:T], src[:, 0:T], ACT.Square).then_inc(sq.sem, 1)

                        def logs(h, j):
                            for g, (a, w) in enumerate(GROUPS):
                                src = B.read(act, h, ("n", j, g))
                                B.release(act.activation(SQ[j][:, a:a + w], src[:, 0:w], ACT.Ln, bias=eps[:]), ("n", j, g))

                        def exps(h, j):
                            for g in range(NG):
                                B.taken(act, h, ("n", j, g))
                            act.activation(SQ[j][:, 0:T], SQ[j][:, 0:T], ACT.Exp, scale=-0.5,
                                           bias=(zero, lnq)[j][:]).then_inc(rn.sem, 1)

                        def scan_chunk(h, c):
                            src = SB.read(act, h, ("u", c))
                            SB.release(act.activation(U[c % 2][:], src[:, 0:P], ACT.Copy), ("u", c))
                            src = SB.read(act, h, ("o", c))
                            SB.release(act.activation(O[:, c * L:c * L + L], src[:, 0:P], ACT.Copy), ("o", c))

                        def out_norms(h):
                            wait(act, osum, h, 2)
                            act.activation(rr[:], ssum[:], ACT.Ln, scale=1.0 / DV_B, bias=eps[:]).then_inc(onorm.sem, 1)
                            wait(act, onorm, h, 1)
                            act.activation(rr[:], rr[:], ACT.Exp, scale=-0.5).then_inc(onorm.sem, 1)

                        def z_gate(h, g, scan):
                            a, w = GROUPS[g]
                            if scan and g == 0:
                                SB.taken(act, h - 1, ("turn", 2))
                            src = B.read(act, h, ("dense", 3, g))
                            B.release(act.activation(ZS[:, a:a + w], src[:, 0:w], ACT.Silu), ("dense", 3, g))

                        def inverse(h):
                            for t in range(3):
                                wait(act, dx, h, t + 1)
                                act.activation(third(DT, t), third(DT, t), ACT.Exp).then_inc(dt.sem, 1)
                            for l in range(1, LEVELS):
                                for t in range(3):
                                    for n, dst in (("d", DM), ("e", E)):
                                        if n == "e" or l < LEVELS - 1:
                                            src = B.read(act, h, (n, l, t))
                                            w = parts(l, t) * L
                                            B.release(act.activation(third(dst, t)[:, 0:w], src[:, 0:w], ACT.Copy), (n, l, t))
                            for t in range(3):
                                src = B.read(act, h, ("wk", t))
                                B.release(act.activation(third(WKT, t), src[:, 0:384], ACT.Copy, scale=-1.0), ("wk", t))

                        def turn(h, scan):
                            for i in range(9):
                                j, g = divmod(i, 3)
                                if scan and i < 8:
                                    scan_chunk(h - 1, i)
                                if g == 0:
                                    halo(h, j)
                                copy_out(h, j, g)
                                if g == 2:
                                    first_tap(h, j)
                                if i in (4, 7):
                                    dst = (KN, QN)[i // 3 - 1]
                                    if scan:
                                        wait(act, qd, h - 1, 1)
                                    silu(h, i // 3 - 1, dst)
                                    squares(h, i // 3 - 1, dst)
                                if scan and i == 8:
                                    scan_chunk(h - 1, i)
                            logs(h, 0)
                            logs(h, 1)
                            exps(h, 0)
                            exps(h, 1)
                            if scan:
                                out_norms(h - 1)
                            silu(h, 2, VS)
                            for g in range(NG):
                                z_gate(h, g, scan)
                            inverse(h)

                        turn(0, False)
                        with act.Fori(1, H_B) as h:
                            turn(h, True)
                        for c in range(NCH):
                            scan_chunk(H_B - 1, c)
                        out_norms(H_B - 1)

                    @block.vector
                    def _(dve):

                        def seq_new(h):
                            dve.tensor_copy(TAPS[:].unsqueeze(2), CT[:, :, bass.ds(h, 1), :])
                            dve.tensor_copy(HG[:].unsqueeze(1), GTB[:, bass.ds(h, 1)]).then_inc(taps.sem, 1)

                        def conv(h, j):
                            for i in range(1, W):
                                if i == 1:
                                    wait(dve, tap0, h, j + 1)
                                else:
                                    wait(dve, cv, h, 3 * j + i - 1)
                                dve.scalar_tensor_tensor(CV[:, 0:CV_LEN], XPB[:, i:i + CV_LEN], TAPS[:, TAP[j], 24 + i:25 + i],
                                                         CV[:, 0:CV_LEN], ALU.mult, ALU.add).then_inc(cv.sem, 1)

                        def unit(h, j, x):
                            wait(dve, rn, h, j + 1)
                            dve.tensor_tensor(x[:, 0:T], x[:, 0:T], SQ[j][:, 0:T], ALU.mult).then_inc(kn.sem, 1)

                        def state(h, c):
                            if c == 0:
                                wait(dve, gl, h, 1)
                            if c < 2 and not (isinstance(h, int) and h == 0):
                                wait(dve, s_st, h - 1, 2)
                            src = SB.read(dve, h, ("s", c))[:, 0:P]
                            if c == 0:
                                ins = dve.tensor_copy(S[1][:], src)
                            else:
                                SB.taken(dve, h, ("s", c - 1))
                                ins = dve.scalar_tensor_tensor(S[(c + 1) % 2][:], S[c % 2][:], GL[:, c:c + 1], src,
                                                               ALU.mult, ALU.add)
                            SB.release(ins, ("s", c))

                        def sample_state(h):
                            SB.taken(dve, h, ("u", NC))
                            dve.tensor_tensor(UM[:, 0:NB * P].rearrange("p (b e) -> p b e", b=NB), over_chunks(U[NC % 2][:], NB),
                                              over_tokens(ohb[:], P), ALU.mult).then_inc(um.sem, 1)
                            SB.read(dve, h, ("o", NC))
                            dve.tensor_tensor(SS[:], SS[:], over_tokens(GL[:, NC:16], P), ALU.mult).then_inc(sgl.sem, 1)
                            wait(dve, sgl, h, 1)
                            for i in range(2):
                                src = SB.read(dve, h, (f"s{i}", NC))
                                v = SS[:, 4 * i:4 * i + 4, :]
                                SB.release(dve.tensor_tensor(v, v, src[:].rearrange("p (b e) -> p b e", b=4), ALU.add), (f"s{i}", NC))

                        def out_sums(h):
                            SB.taken(dve, h, ("o", NC))
                            dve.tensor_tensor(SQO[:], O[:], O[:], ALU.mult).then_inc(osum.sem, 1)
                            wait(dve, osum, h, 1)
                            dve.tensor_reduce(ssum[:], chunks(SQO[:]), AX_X, ALU.add).then_inc(osum.sem, 1)

                        def out_scale(h):
                            wait(dve, onorm, h, 2)
                            dve.tensor_tensor(chunks(O[:]), chunks(O[:]), over_tokens(rr[:]), ALU.mult).then_inc(oscaled.sem, 1)

                        def out_gate(h):
                            for t, (a, w) in enumerate(GROUPS):
                                src = SB.read(dve, h, ("turn", t))
                                SB.release(dve.scalar_tensor_tensor(HBT[:, a:a + w], src[:, 0:w], gbh[:], ZS[:, a:a + w],
                                                                    ALU.mult, ALU.mult), ("turn", t))

                        def inverse(h, scan):
                            wait(dve, s_row[0], h, 1)
                            wait(dve, kn, h, 2)
                            wait(dve, taps, h, 1)
                            for c in range(NCH):
                                ins = dve.scalar_tensor_tensor(DT[:, c * L:c * L + L], GAM[:, c * L:c * L + L], HG[:, 0, c:c + 1],
                                                               (madd if c < NC else madds)[:], ALU.add, ALU.add)
                                if c % 3 == 2:
                                    ins.then_inc(dx.sem, 1)
                            wait(dve, s_row[1], h, 1)
                            dve.tensor_copy(GL[:, 0:NC], chunks(EG[:])[:, 0:NC, L - 1])
                            dve.tensor_copy(GL[:, NC:16], sequences(EG)[:, :, NS - 1]).then_inc(gl.sem, 1)
                            if scan:
                                wait(dve, s_hb, h - 1, 1)
                            for t in range(3):
                                s = slice(3 * t, 3 * t + 3)
                                src = three(B.read(dve, h, ("kt", t))[:, 0:384])
                                dve.tensor_tensor(three(third(KD, t)), src, over_tokens(HG[:, 1, s]), ALU.mult)
                                B.release(dve.tensor_tensor(three(third(KBE, t)), src, over_tokens(HG[:, 3, s]), ALU.mult), ("kt", t))
                                src = three(B.read(dve, h, ("vt", t))[:, 0:384])
                                B.release(dve.tensor_tensor(three(third(BV, t)), src, over_tokens(HG[:, 2, s]), ALU.mult), ("vt", t))
                                wait(dve, dt, h, t + 1)
                                for n, dst in (("p1", AT), ("p2", QKT)):
                                    src = B.read(dve, h, (n, t))
                                    B.release(dve.tensor_tensor(third(dst, t), src[:, 0:384], third(DT, t), ALU.mult), (n, t))
                            for t in range(3):
                                src = three(B.read(dve, h, ("at", t))[:, 0:384])
                                B.release(dve.tensor_tensor(three(third(DM, t)), src, over_chunks(SM[:, 0, :]), ALU.mult), ("at", t))
                            for l in range(1, LEVELS):
                                for t in range(3):
                                    n = parts(l, t)
                                    src = B.read(dve, h, ("z", l, t))[:, 0:n * L].rearrange("p (c t) -> p c t", c=n)
                                    B.release(dve.tensor_tensor(three(third(Z, t))[:, 0:n], src, over_chunks(SM[:, l, :], n),
                                                                ALU.mult), ("z", l, t))
                            B.taken(dve, h, ("wk", 2))
                            wait(dve, qd, h, 1)
                            dve.tensor_copy(blocks(WKM), sequences(WKT))
                            dve.tensor_copy(blocks(QDM), sequences(QD)).then_inc(masked.sem, 1)

                        def turn(h, scan, nxt):
                            seq_new(h)
                            for i in range(12):
                                if i % 3 == 0 and i < 9:
                                    WS.split_hi(dve, h, i // 3 + 1, B)
                                if i == 9 and nxt:
                                    WS.split_hi(dve, h + 1, 0, B)
                                if scan:
                                    if i < NC:
                                        state(h - 1, i)
                                    elif i == NC:
                                        sample_state(h - 1)
                                    elif i == 9:
                                        out_sums(h - 1)
                                if i in (3, 6, 9):
                                    conv(h, i // 3 - 1)
                                if i == 10:
                                    unit(h, 0, KN)
                                    unit(h, 1, QN)
                                    if scan:
                                        out_scale(h - 1)
                                        out_gate(h - 1)
                            inverse(h, scan)

                        WS.split_hi(dve, 0, 0, B)
                        dve.wait_ge(s_gb, 16)
                        dve.tensor_scalar(gbh[:], gb[:], 0.5, None, ALU.mult).then_inc(half.sem, 1)
                        wait(dve, half, 0, 1)
                        dve.wait_ge(s_mask, MASKS)
                        turn(0, False, True)
                        with dve.Fori(1, H_B - 1) as h:
                            turn(h, True, True)
                        turn(H_B - 1, True, False)
                        for c in range(NC):
                            state(H_B - 1, c)
                        sample_state(H_B - 1)
                        out_sums(H_B - 1)
                        out_scale(H_B - 1)
                        out_gate(H_B - 1)

        def mlstm():
            NJ = 6
            E1 = DV_A + 1
            dense = [("dense", j, g) for j in range(NJ) for g in range(NG)]
            mats = [(n, t) for t in range(3) for n in ("kt", "va", "vb", "p")]
            scan = [(n, c) for c in range(NC) for n in ("c", "num")] + [("num", NC)] + [("cs", b) for b in range(NB)]
            turn_ = [(n, t) for t in range(3) for n in ("ta", "tb")]
            B = Banks(psum[0:6], dense + mats, sem, "a_main")
            SB = Banks(psum[6:8], scan + turn_, sem, "a_scan")
            with ExitStack() as st:
                sb = sbuf_in(st)
                WS = Weights(sb, sem, "a_w", per=NJ)
                K, Q, V0, V1 = (sb(n, [P, TP]) for n in ("a_k", "a_q", "a_v0", "a_v1"))
                OG = [sb(f"a_o{i}", [P, T]) for i in range(2)]
                ROW, WIN = sb("a_row", [P, TP]), sb("a_win", [P, TP])
                DECS = sb("a_dec", [P, 16])
                ST = sb("a_st", [P, TP])
                KW = sb("a_kw", [P, TP])
                VT = sb("a_vt", [P, NCH, E1])
                NUM = sb("a_num", [P, NCH, E1])
                C = [sb(f"a_c{i}", [P, E1]) for i in range(2)]
                CS = sb("a_cs", [P, NB, E1])
                QM = sb("a_qm", [P, NB * (P + NS)])
                VM = sb("a_vm", [P, NB, E1])
                HG = sb("a_hg", [P, 3, NCH])
                ga = sb("a_ga", [P, H_A * 2])
                GH = sb("a_gh", [P, 2])
                SQN = sb("a_sqn", [P, NCH, DV_A])
                ssum, den, rr = sb("a_ssum", [P, NCH]), sb("a_den", [P, NCH]), sb("a_rr", [P, NCH])
                HT = [V0, V1]
                NL = 7
                s_init, s_ga = sem("a_init"), sem("a_ga_landed")
                s_row = [landed(f"a_row{i}_landed") for i in range(3)]
                s_cs = landed("a_cs_landed", 2)
                s_st = landed("a_state_stored", 4)
                s_ha = landed("a_out_stored", 2)
                hg = event("a_scalars_ready")
                dx, dw, qi = event("a_exponents", 3), event("a_weights", 3), event("a_q_decayed")
                qm, vm, csd = event("a_qm_ready"), event("a_vm_ready"), event("a_cs_decayed")
                fin = event("a_fin_step", NL)
                lnr = event("a_norms", 2)
                hsc, og = event("a_scaled"), event("a_gate_ready")

                def sequences(ap):
                    return ap[:, SEQ:T].rearrange("p (b t) -> p b t", t=NS)

                def offset(h, j):
                    return (h * P + O_K, h * P + O_Q, h * 2 * P + O_V, h * 2 * P + O_V + P, h * 2 * P + O_O,
                            h * 2 * P + O_O + P)[j]

                with nc.Block() as block:
                    @block.sync
                    def _(sp):
                        def slab(h, j):
                            e = 8 if j == 1 else 1
                            o = offset(h, j) if e == 1 else h * (P // e) + O_Q // e
                            WS.load(sp, h, j, win.rearrange("k (x e) -> k x e", e=e)[:, bass.ds(o, P // e), :])

                        def turn(h, later, nxt):
                            if later:
                                stores(h - 1)
                            for i, (dst, src) in enumerate(((ROW, ROWS_A[bass.ds(h, 1), 0]), (WIN, ROWS_A[bass.ds(h, 1), 1]),
                                                            (DECS, DECS_A[bass.ds(h, 1)]))):
                                sp.dma_start(dst[:], src.to_broadcast([P, dst.shape[1]])).then_inc(s_row[i].sem, 16)
                            sp.dma_start(CS[:, :, 0:DV_A], state_C[0, :, bass.ds(h, 1)].rearrange("b a k v -> k (b a) v")).then_inc(s_cs.sem, 16)
                            sp.dma_start(CS[:, :, DV_A:E1], state_n[0, :, bass.ds(h, 1)].rearrange("b a k -> k b a")).then_inc(s_cs.sem, 16)
                            for j in range(3, NJ):
                                slab(h, j)
                            if nxt:
                                for j in range(3):
                                    slab(h + 1, j)

                        def stores(h):
                            SB.taken(sp, h, ("cs", NB - 2))
                            c = C[NC % 2]
                            sp.dma_start(C_prompt[0, 0, bass.ds(h, 1)].rearrange("a k v -> k (a v)"), c[:, 0:DV_A]).then_inc(s_st.sem, 16)
                            sp.dma_start(n_prompt[0, 0, bass.ds(h, 1)].rearrange("a k -> k a"), c[:, DV_A:E1]).then_inc(s_st.sem, 16)
                            SB.taken(sp, h, ("cs", NB - 1))
                            sp.dma_start(C_sample[0, :, bass.ds(h, 1)].rearrange("b a k v -> k (b a) v"), CS[:, :, 0:DV_A]).then_inc(s_st.sem, 16)
                            sp.dma_start(n_sample[0, :, bass.ds(h, 1)].rearrange("b a k -> k b a"), CS[:, :, DV_A:E1]).then_inc(s_st.sem, 16)
                            for i, n in enumerate(("ta", "tb")):
                                SB.taken(sp, h, (n, 2))
                                sp.dma_start(HA[bass.ds(h, 1), i].rearrange("a p t -> p (a t)"), HT[i][:, 0:T]).then_inc(s_ha.sem, 16)
                            wait(sp, s_st, h, 4)

                        slab(0, 0)
                        sp.dma_start(ga[:], g_norm_a[0].rearrange("(m p) -> p m", p=P)).then_inc(s_ga, 16)
                        for j in range(1, 3):
                            slab(0, j)
                        turn(0, False, True)
                        with sp.Fori(1, H_A - 1) as h:
                            turn(h, True, True)
                        turn(H_A - 1, True, False)
                        stores(H_A - 1)
                        wait(sp, s_ha, H_A - 1, 2)

                    @block.gpsimd
                    def _(pool):
                        WS.split_lo(pool, 0, 0)
                        for x in (K, Q, V0, V1):
                            pool.memset(x[:, T:TP], 0.0).then_inc(s_init, 1)
                        pool.memset(QM[:], 0.0).then_inc(s_init, 1)
                        pool.memset(VT[:, :, DV_A:E1], 1.0).then_inc(s_init, 1)

                        def turn(h, nxt):
                            for j in range(3, NJ):
                                WS.split_lo(pool, h, j)
                            if nxt:
                                for j in range(3):
                                    WS.split_lo(pool, h + 1, j)

                        for j in range(1, 3):
                            WS.split_lo(pool, 0, j)
                        turn(0, True)
                        with pool.Fori(1, H_A - 1) as h:
                            turn(h, True)
                        turn(H_A - 1, False)

                    @block.tensor
                    def _(pe):
                        def group(h, j, g):
                            a, w = GROUPS[g]
                            slot = ("dense", j, g)
                            if g == 0:
                                WS.ready(pe, h, j)
                            bank = B.claim(pe, h, slot)
                            B.filled(WS.product(pe, j, bank[:, 0:w], hhi[:, :, a:a + w], hlo[:, :, a:a + w]), slot)

                        def turned(h, slot, x, need):
                            t = slot[1]
                            bank = B.claim(pe, h, slot, *need)
                            for i in range(3):
                                a = (3 * t + i) * L
                                ins = pe.transpose(bank[:, i * L:i * L + L], x[:, a:a + L], ident[:])
                            B.filled(ins, slot)

                        def matrices(h):
                            for t in range(3):
                                turned(h, ("kt", t), K, [("dense", 0, min(t, 2))])
                                turned(h, ("va", t), V0, [("dense", 2, t)])
                                turned(h, ("vb", t), V1, [("dense", 3, t)])
                                bank = B.claim(pe, h, ("p", t), ("dense", 1, t))
                                for i in range(3):
                                    a = (3 * t + i) * L
                                    ins = pe.matmul(bank[:, i * L:i * L + L], K[:, a:a + L], Q[:, a:a + L], start=True, stop=True)
                                B.filled(ins, ("p", t))

                        def scan_all(h):
                            for c in range(NC):
                                a = c * L
                                if c % 3 == 0:
                                    for n in ("kt", "va", "vb", "p"):
                                        B.taken(pe, h, (n, c // 3))
                                if c == 1:
                                    wait(pe, qi, h, 1)
                                bank = SB.claim(pe, h, ("c", c))
                                SB.filled(pe.matmul(bank[:, 0:E1], KW[:, a:a + L], VT[:, c, :], start=True, stop=True), ("c", c))
                                bank = SB.claim(pe, h, ("num", c), *([("c", c - 1)] if c else []))
                                ins = pe.matmul(bank[:, 0:E1], ST[:, a:a + L], VT[:, c, :], start=True, stop=(c == 0))
                                if c:
                                    ins = pe.matmul(bank[:, 0:E1], Q[:, a:a + L], C[c % 2][:], start=False, stop=True)
                                SB.filled(ins, ("num", c))
                            a = NC * L
                            bank = SB.claim(pe, h, ("num", NC))
                            wait(pe, s_cs, h, 2)
                            wait(pe, qm, h, 1)
                            pe.matmul(bank[:, 0:E1], ST[:, a:a + L], VT[:, NC, :], start=True, stop=False)
                            for b in range(NB):
                                ins = pe.matmul(bank[:, 0:E1], QM[:, P * b:P * b + P], CS[:, b, :], start=False, stop=(b == NB - 1))
                            SB.filled(ins, ("num", NC))
                            wait(pe, vm, h, 1)
                            for b in range(NB):
                                bank = SB.claim(pe, h, ("cs", b))
                                SB.filled(pe.matmul(bank[:, 0:E1], KW[:, a:a + L], VM[:, b, :], start=True, stop=True), ("cs", b))

                        def outputs(h):
                            wait(pe, hsc, h, 1)
                            for t in range(3):
                                for n, e in (("ta", 0), ("tb", P)):
                                    bank = SB.claim(pe, h, (n, t))
                                    for i in range(3):
                                        ins = pe.transpose(bank[:, i * L:i * L + L], NUM[:, 3 * t + i, e:e + P], ident[:])
                                    SB.filled(ins, (n, t))

                        def turn(h, nxt):
                            for j in range(1, NJ):
                                for g in range(NG):
                                    group(h, j, g)
                            matrices(h)
                            scan_all(h)
                            if nxt:
                                for g in range(NG):
                                    group(h + 1, 0, g)
                            outputs(h)

                        for g in range(NG):
                            group(0, 0, g)
                        pe.wait_ge(s_init, 6)
                        with pe.Fori(0, H_A - 1) as h:
                            turn(h, True)
                        turn(H_A - 1, False)

                    @block.scalar
                    def _(act):
                        def copy_out(h, j, g):
                            a, w = GROUPS[g]
                            src = B.read(act, h, ("dense", j, g))[:, 0:w]
                            if j < 4:
                                ins = act.activation((K, Q, V0, V1)[j][:, a:a + w], src, ACT.Copy, scale=DK ** -0.5 if j == 1 else 1.0)
                            else:
                                ins = act.activation(OG[j - 4][:, a:a + w], src, ACT.Tanh, scale=0.5)
                            B.release(ins, ("dense", j, g))

                        def turn(h, later):
                            for j in range(NJ):
                                for g in range(NG):
                                    if later and g == 0 and j == 2:
                                        wait(act, s_ha, h - 1, 2)
                                    copy_out(h, j, g)
                            for t in range(3):
                                wait(act, dx, h, t + 1)
                                act.activation(third(ST, t), third(ST, t), ACT.Exp).then_inc(dw.sem, 1)
                            for c in range(NCH):
                                src = SB.read(act, h, ("num", c))
                                SB.release(act.activation(NUM[:, c, :], src[:, 0:E1], ACT.Copy), ("num", c))
                            wait(act, fin, h, NL - 1)
                            act.activation(rr[:], rr[:], ACT.Ln).then_inc(lnr.sem, 1)
                            wait(act, lnr, h, 1)
                            act.activation(rr[:], rr[:], ACT.Exp, scale=-0.5).then_inc(lnr.sem, 1)

                        turn(0, False)
                        with act.Fori(1, H_A) as h:
                            turn(h, True)

                    @block.vector
                    def _(dve):
                        def matrices(h):
                            dve.tensor_copy(HG[:].unsqueeze(1), GTA[:, bass.ds(h, 1)])
                            dve.tensor_scalar(GH[:].unsqueeze(1), ga[:].rearrange("p (h e) -> p h e", e=2)[:, bass.ds(h, 1), :], 0.25, None,
                                              ALU.mult).then_inc(hg.sem, 1)
                            wait(dve, hg, h, 1)
                            wait(dve, s_row[0], h, 1)
                            for c in range(NCH):
                                ins = dve.scalar_tensor_tensor(ST[:, c * L:c * L + L], ROW[:, c * L:c * L + L], HG[:, 0, c:c + 1],
                                                               (madd if c < NC else madds)[:], ALU.add, ALU.add)
                                if c % 3 == 2:
                                    ins.then_inc(dx.sem, 1)
                            for t in range(3):
                                s = slice(3 * t, 3 * t + 3)
                                src = three(B.read(dve, h, ("kt", t))[:, 0:384])
                                B.release(dve.tensor_tensor(three(third(KW, t)), src, over_tokens(HG[:, 1, s]), ALU.mult), ("kt", t))
                                for n, e in (("va", 0), ("vb", P)):
                                    src = three(B.read(dve, h, (n, t))[:, 0:384])
                                    B.release(dve.tensor_copy(VT[:, s, e:e + P], src), (n, t))
                                wait(dve, dw, h, t + 1)
                                src = B.read(dve, h, ("p", t))
                                B.release(dve.tensor_tensor(third(ST, t), src[:, 0:384], third(ST, t), ALU.mult), ("p", t))
                            wait(dve, s_row[1], h, 1)
                            dve.tensor_tensor(Q[:], Q[:], WIN[:], ALU.mult).then_inc(qi.sem, 1)
                            wait(dve, qi, h, 1)
                            dve.tensor_copy(QM[:].rearrange("p (b x) -> p b x", x=P + NS)[:, :, 0:NS], sequences(Q)).then_inc(qm.sem, 1)

                        def scan_all(h, later):
                            wait(dve, s_row[2], h, 1)
                            if later:
                                wait(dve, s_st, h - 1, 4)
                            for c in range(NC):
                                src = SB.read(dve, h, ("c", c))[:, 0:E1]
                                if c == 0:
                                    ins = dve.tensor_copy(C[1][:], src)
                                else:
                                    SB.taken(dve, h, ("c", c - 1))
                                    ins = dve.scalar_tensor_tensor(C[(c + 1) % 2][:], C[c % 2][:], DECS[:, c:c + 1], src,
                                                                   ALU.mult, ALU.add)
                                SB.release(ins, ("c", c))
                            for t in range(3):
                                B.taken(dve, h, ("va", t))
                                B.taken(dve, h, ("vb", t))
                            dve.tensor_tensor(VM[:], over_chunks(VT[:, NC, :], NB), over_tokens(ohb[:], E1), ALU.mult).then_inc(vm.sem, 1)
                            SB.read(dve, h, ("num", NC))
                            dve.tensor_tensor(CS[:], CS[:], over_tokens(DECS[:, NC:16], E1), ALU.mult).then_inc(csd.sem, 1)
                            wait(dve, csd, h, 1)
                            for b in range(NB):
                                src = SB.read(dve, h, ("cs", b))[:, 0:E1]
                                SB.release(dve.tensor_tensor(CS[:, b, :], CS[:, b, :], src, ALU.add), ("cs", b))

                        def step(h, n, ins):
                            ins.then_inc(fin.sem, 1)
                            wait(dve, fin, h, n)

                        def finish(h, nxt):
                            SB.taken(dve, h, ("num", NC))
                            step(h, 1, dve.tensor_tensor(SQN[:], NUM[:, :, 0:DV_A], NUM[:, :, 0:DV_A], ALU.mult))
                            step(h, 2, dve.scalar_tensor_tensor(den[:], NUM[:, :, DV_A], -1.0, NUM[:, :, DV_A], ALU.mult, ALU.max))
                            step(h, 3, dve.tensor_tensor(den[:], den[:], HG[:, 2, :], ALU.max))
                            step(h, 4, dve.tensor_reduce(ssum[:], SQN[:], AX_X, ALU.add))
                            step(h, 5, dve.scalar_tensor_tensor(den[:], den[:], DV_A * EPS, den[:], ALU.mult, ALU.mult))
                            step(h, 6, dve.tensor_tensor(rr[:], ssum[:], den[:], ALU.add))
                            step(h, 7, dve.tensor_scalar(GH[:], GH[:], float(DV_A) ** 0.5, None, ALU.mult))
                            wait(dve, lnr, h, 2)
                            dve.tensor_tensor(NUM[:, :, 0:DV_A], NUM[:, :, 0:DV_A], over_tokens(rr[:], DV_A), ALU.mult).then_inc(hsc.sem, 1)
                            if nxt:
                                WS.split_hi(dve, h + 1, 2, B)
                            for i in range(2):
                                B.taken(dve, h, ("dense", 4 + i, NG - 1))
                            for i in range(2):
                                ins = dve.tensor_scalar(OG[i][:], OG[i][:], 1.0, GH[:, i:i + 1], ALU.add, ALU.mult)
                            ins.then_inc(og.sem, 1)
                            wait(dve, og, h, 1)
                            for t, (a, w) in enumerate(GROUPS):
                                for i, n in enumerate(("ta", "tb")):
                                    src = SB.read(dve, h, (n, t))[:, 0:w]
                                    SB.release(dve.tensor_tensor(HT[i][:, a:a + w], src, OG[i][:, a:a + w], ALU.mult), (n, t))

                        def turn(h, later, nxt):
                            for j in range(3, NJ):
                                WS.split_hi(dve, h, j, B)
                            if nxt:
                                WS.split_hi(dve, h + 1, 0, B)
                                WS.split_hi(dve, h + 1, 1, B)
                            matrices(h)
                            scan_all(h, later)
                            finish(h, nxt)

                        for j in range(3):
                            WS.split_hi(dve, 0, j, B)
                        dve.wait_ge(s_ga, 16)
                        turn(0, False, True)
                        with dve.Fori(1, H_A - 1) as h:
                            turn(h, True, True)
                        turn(H_A - 1, True, False)

        def tail():
            NBLK, HALF = F_FF // D, KT // 2
            S_A, S_B = 0, KT
            S_OUT = 2 * KT
            S_FFN = S_OUT + HALF
            S_LAST = S_FFN + 2 * HALF * (NBLK - 1)
            S_PLE = S_FFN + 2 * HALF * NBLK
            S_END = S_PLE + KT
            dense = [("dense", j, g) for j in range(2) for g in range(NG)]
            B = Banks(psum[0:6], dense, sem, "t_main")
            sums = [("sum", i, g) for i in range(2) for g in range(NG)]
            NQ = 3 * H_B // 4
            SB = Banks(psum[6:8], [("co", q) for q in range(NQ)] + sums + [("p", t) for t in range(6)] + [("token", 2)],
                       sem, "t_side")
            with ExitStack() as st:
                sb = sbuf_in(st)
                WS = Weights(sb, sem, "t_w", per=2)
                rhi = sb("t_rhi", [P, KT, T], F32R)
                with ExitStack() as alias:
                    rraw = sbuf_in(alias)("t_rraw", [P, KT, T])
                rlo = sb("t_rlo", [P, KT, T], F32R)
                XM = sb("t_x", [P, KT, T])
                GR = sb("t_gr", [P, T])
                V = sb("t_v", [P, T])
                ACC = sb("t_acc", [P, T])
                gf, gp, gl_ = sb("t_gf", [P, KT]), sb("t_gp", [P, KT]), sb("t_gfin", [P, KT])
                NHI, NLO = rhi, rlo
                UHI, ULO = hhi, hlo
                flat_hi, flat_lo = hraw[:, 0:KT * T], hraw[:, KT * T:2 * KT * T]
                prow = flat_hi[:, 0:NCH * PLE].rearrange("p (c e) -> p c e", e=PLE)
                PHI, PLO = hlo[:, 0:2, :], hlo[:, 2:4, :]
                ACC2, V2, SG = (flat_lo[:, T * i:T * i + T] for i in (4, 5, 6))

                crows = XM[0:27, 5:KT, :].rearrange("p k t -> p (k t)")
                RT = sb("t_rt", [P, NCH])

                def yrow(c):
                    return flat_hi[:, D * c:D * c + D] if c < NC else flat_lo[:, 5 * T:5 * T + D]

                s_g = sem("t_gains_landed")
                s_br = [landed(f"t_branch{i}_landed") for i in range(4)]
                bhi, blo = event("t_branch_hi", KT), event("t_branch_lo", 4)
                blod = event("t_branch_lo_dve", 4)
                mixed = event("t_mix_product", NG)
                mhi, mlo, mlop = event("t_mix_hi"), event("t_mix_lo"), event("t_mix_lo_pool")
                s_x = [landed(f"t_x{i}_landed") for i in range(2)]
                nhi_ = [event(f"t_n{i}_hi", KT) for i in range(2)]
                nlo_ = [event(f"t_n{i}_lo", KT) for i in range(2)]
                sq_ = [event(f"t_square{i}", KT) for i in range(3)]
                acc_ = [event(f"t_squares_added{i}", KT - 1) for i in range(3)]
                rms = event("t_rms", NG)
                rsq, uhi, ulo = (event(n, KT * NG) for n in ("t_relu_squared", "t_u_hi", "t_u_lo"))
                s_p = landed("t_p_landed", 2)
                phi = event("t_p_hi", 6)
                gsig = event("t_gate_sig", NG)
                upd = event("t_update", NG)
                y = event("t_y", KT)
                rt = event("t_final_rms", 4)
                s_co = landed("t_conv_stored", 2)
                s_y = landed("t_y_stored", NCH)

                with nc.Block() as block:
                    @block.sync
                    def _(sp):
                        def branch(i, src):
                            for q in range(4):
                                sp.dma_start(rraw[:, 2 * q:2 * q + 2, :],
                                             src[2 * q:2 * q + 2].rearrange("k p t -> p k t")).then_inc(s_br[q].sem, 16)

                        def pair(s, m, o, w):
                            e = 8
                            WS.load(sp, s, 0, win.rearrange("k (x e) -> k x e", e=e)[:, bass.ds(m * (P // e) + o // e, P // e), :])
                            WS.load(sp, s, 1, slab_of(w[0], m))

                        def square(s, u, w):
                            for j in range(2):
                                WS.load(sp, s, j, slab_of(w, u, j, 2))

                        pair(0, 0, O_GA, w_pa)
                        branch(0, HA.rearrange("h i p t -> (h i) p t"))
                        for t_, v in ((gf, g_ffn[0]), (gp, g_ple[0]), (gl_, g_final)):
                            sp.dma_start(t_[:], v.rearrange("(k p) -> p k", p=P)).then_inc(s_g, 16)
                        for q in (NQ - 2, NQ - 1):
                            SB.taken(sp, 0, ("co", q))
                        sp.dma_start(conv_prompt[0, 0], crows[0:HALO, 0:3 * H_B * P]).then_inc(s_co.sem, 16)
                        sp.dma_start(conv_sample[0].rearrange("b j c -> (b j) c"), crows[HALO:27, 0:3 * H_B * P]).then_inc(s_co.sem, 16)
                        with sp.Fori(1, KT) as m:
                            pair(m, m, O_GA, w_pa)
                        WS.load(sp, S_B, 0, win[:, O_GB:O_GB + P])
                        B.read(sp, S_B - 1, ("dense", 1, NG - 1))
                        branch(1, HB)
                        WS.load(sp, S_B, 1, w_pb[0][:, 0:P])
                        with sp.Fori(S_B + 1, S_OUT) as s:
                            pair(s, s - S_B, O_GB, w_pb)
                        square(S_OUT, 0, w_out[0])
                        wait(sp, mlo, 0, KT // 2 - 1)
                        wait(sp, mlop, 0, KT // 2)
                        sp.dma_start(XM[:, 0:KT - 1, :], XT[0:KT - 1].rearrange("k p t -> p k t")).then_inc(s_x[0].sem, 16)
                        wait(sp, mlo, 0, KT // 2 - 1 + NG)
                        sp.dma_start(XM[:, KT - 1, :], XT[KT - 1]).then_inc(s_x[1].sem, 16)
                        with sp.Fori(S_OUT + 1, S_FFN) as s:
                            square(s, s - S_OUT, w_out[0])
                        with sp.Fori(0, NBLK) as f:
                            for u in range(HALF):
                                for j in range(2):
                                    WS.load(sp, f * (2 * HALF) + (S_FFN + u), j, slab_of(w_up[0], f, 2 * u + j, KT))
                            for u in range(HALF):
                                for j in range(2):
                                    m = 2 * u + j
                                    WS.load(sp, f * (2 * HALF) + (S_FFN + HALF + u), j, w_down[0][bass.ds(f * D, D), m * P:m * P + P])
                        for m in range(KT):
                            WS.load(sp, S_PLE + m, 0, w_pg[0][:, m * P:m * P + P])
                            if m == 0:
                                B.read(sp, S_PLE - 1, ("dense", 1, NG - 1))
                                sp.dma_start(prow[:, 0:NC, :], p_prompt[0, 0].rearrange("(c p) e -> p c e", p=P)).then_inc(s_p.sem, 16)
                                sp.dma_start(prow[0:NB * NS, NC, :], p_sample[0].rearrange("b t e -> (b t) e")).then_inc(s_p.sem, 16)
                            WS.load(sp, S_PLE + m, 1, w_pp[0][:, m * P:m * P + P], kt=PLE // P)
                        for c in range(NCH):
                            for u in range(2):
                                B.taken(sp, S_END + c // 3, dense[2 * (c % 3) + u])
                            if c < NC:
                                sp.dma_start(y_prompt[0, c * L:c * L + L, :], yrow(c)).then_inc(s_y.sem, 16)
                            else:
                                sp.dma_start(y_sample.rearrange("b t d -> (b t) d"), yrow(c)[0:NB * NS, :]).then_inc(s_y.sem, 16)
                        wait(sp, s_y, 0, NCH)
                        wait(sp, s_co, 0, 2)

                    @block.gpsimd
                    def _(pool):
                        def branch(i):
                            for k in range(0, KT, 2):
                                wait(pool, bhi, i, k + 1)
                                pool.tensor_tensor(NLO[:, k, :], rraw[:, k, :], NHI[:, k, :], ALU.subtract).then_inc(blo.sem, 1)

                        def squares(i, m):
                            acc = ACC2 if i == 2 else ACC[:]
                            if m:
                                wait(pool, sq_[i], 0, m + 1)
                                if m > 1:
                                    wait(pool, acc_[i], 0, m - 1)
                                pool.tensor_tensor(acc, acc, V[:], ALU.add).then_inc(acc_[i].sem, 1)

                        WS.split_lo(pool, 0, 0)
                        WS.split_lo(pool, 0, 1)
                        branch(0)
                        with pool.Fori(1, KT) as s:
                            WS.split_lo(pool, s, 0)
                            WS.split_lo(pool, s, 1)
                        WS.split_lo(pool, S_B, 0)
                        branch(1)
                        WS.split_lo(pool, S_B, 1)
                        with pool.Fori(S_B + 1, S_OUT) as s:
                            WS.split_lo(pool, s, 0)
                            WS.split_lo(pool, s, 1)
                        WS.split_lo(pool, S_OUT, 0)
                        for k in range(0, KT, 2):
                            wait(pool, mhi, 0, k + 1)
                            pool.tensor_tensor(ULO[:, k, :], XM[:, k, :], UHI[:, k, :], ALU.subtract).then_inc(mlop.sem, 1)
                        for s in range(S_OUT, S_FFN):
                            for j in range(2):
                                n = 2 * s + j + 1
                                WS.split_lo(pool, n // 2, n % 2)
                                squares(0, n - 1 - 2 * S_OUT)
                        with pool.Fori(S_FFN, S_LAST + HALF) as s:
                            WS.split_lo(pool, s, 1)
                            WS.split_lo(pool, s + 1, 0)
                        for s in range(S_LAST + HALF, S_PLE):
                            for j in range(2):
                                n = 2 * s + j + 1
                                WS.split_lo(pool, n // 2, n % 2)
                                squares(1, n - 1 - 2 * (S_LAST + HALF))
                        for m in range(KT):
                            WS.split_lo(pool, S_PLE + m, 1, kt=PLE // P)
                            if m < KT - 1:
                                WS.split_lo(pool, S_PLE + m + 1, 0)
                            squares(2, m)

                    @block.tensor
                    def _(pe):
                        def group(s, j, g, hi, lo, kt=KT):
                            a, w = GROUPS[g]
                            slot = ("dense", j, g)
                            if g == 0:
                                WS.ready(pe, s, j)
                            bank = B.claim(pe, s, slot)
                            B.filled(WS.product(pe, j, bank[:, 0:w], hi[:, :, a:a + w], lo[:, :, a:a + w], kt=kt), slot)

                        def slab(s, j, hi, lo, kt=KT):
                            for g in range(NG):
                                group(s, j, g, hi, lo, kt)

                        def summed(i):
                            wait(pe, acc_[i], 0, KT - 1)
                            for g, (a, w) in enumerate(GROUPS):
                                bank = SB.claim(pe, 0, ("sum", i, g))
                                SB.filled(pe.matmul(bank[:, 0:w], ones[:], ACC[:, a:a + w], start=True, stop=True), ("sum", i, g))

                        def first(s, j, i):
                            wait(pe, nlo_[i], 0, KT)
                            for g in range(NG):
                                group(s, j, g, NHI, NLO)
                                if g == 1:
                                    summed(i)

                        def branch(i, s0):
                            slab(s0, 0, hhi, hlo)
                            wait(pe, blo, i, 4)
                            wait(pe, blod, i, 4)
                            slab(s0, 1, NHI, NLO)
                            with pe.Fori(s0 + 1, s0 + KT) as s:
                                slab(s, 0, hhi, hlo)
                                slab(s, 1, NHI, NLO)

                        for q in range(NQ):
                            bank = SB.claim(pe, 0, ("co", q))
                            for i in range(4):
                                ins = pe.transpose(bank[0:27, i * P:i * P + P], CO[:].rearrange("p a b r -> p (a b) r")[:, 4 * q + i, :],
                                                   ident[:])
                            SB.filled(ins, ("co", q))
                        branch(0, S_A)
                        branch(1, S_B)
                        wait(pe, mlop, 0, KT // 2)
                        for g in range(NG):
                            wait(pe, mlo, 0, KT // 2 + g)
                            group(S_OUT, 0, g, UHI, ULO)
                        slab(S_OUT, 1, UHI, ULO)
                        with pe.Fori(S_OUT + 1, S_FFN) as s:
                            for j in range(2):
                                slab(s, j, UHI, ULO)

                        def block_(f, lead):
                            s = f * (2 * HALF) + S_FFN
                            for u in range(HALF):
                                for j in range(2):
                                    if lead and u == 0 and j == 0:
                                        first(s, 0, 0)
                                    else:
                                        slab(s + u, j, NHI, NLO)
                            wait(pe, ulo, f, KT * NG)
                            for u in range(HALF):
                                for j in range(2):
                                    slab(s + HALF + u, j, UHI, ULO)

                        block_(0, True)
                        with pe.Fori(1, NBLK) as f:
                            block_(f, False)
                        first(S_PLE, 0, 1)
                        wait(pe, s_p, 0, 2)
                        for t in range(6):
                            e, q = t % 2, t // 2
                            bank = SB.claim(pe, 0, ("p", t))
                            for i in range(3):
                                c = 3 * q + i
                                w = L if c < NC else NB * NS
                                ins = pe.transpose(bank[:, i * L:i * L + w], prow[0:w, c, e * P:e * P + P], ident[0:w, 0:w])
                            SB.filled(ins, ("p", t))
                        for m in range(KT):
                            s = S_PLE + m
                            if m:
                                slab(s, 0, NHI, NLO)
                            else:
                                for b in range(2):
                                    SB.taken(pe, 0, ("p", 4 + b))
                            slab(s, 1, PHI, PLO, kt=PLE // P)
                        wait(pe, y, 0, KT)
                        for c in range(NCH):
                            w = L if c < NC else NB * NS
                            if c == 3:
                                wait(pe, acc_[2], 0, KT - 1)
                                bank = SB.claim(pe, 0, ("token", 2))
                                for i in range(NCH):
                                    n = L if i < NC else NB * NS
                                    ins = pe.matmul(bank[0:n, i:i + 1], ACC2[:, i * L:i * L + n], ones[:, 0:1], start=True, stop=True)
                                SB.filled(ins, ("token", 2))
                            for u in range(2):
                                slot = dense[2 * (c % 3) + u]
                                bank = B.claim(pe, S_END + c // 3, slot)
                                for k in range(4):
                                    ins = pe.transpose(bank[0:w, k * P:k * P + P], XM[:, 4 * u + k, c * L:c * L + w], ident[:])
                                B.filled(ins, slot)

                    @block.scalar
                    def _(act):
                        def gate(s, later=True):
                            for g, (a, w) in enumerate(GROUPS):
                                if later:
                                    B.taken(act, s - 1, ("dense", 1, g))
                                src = B.read(act, s, ("dense", 0, g))
                                B.release(act.activation(GR[:, a:a + w], src[:, 0:w], ACT.Tanh, scale=0.5), ("dense", 0, g))

                        def square(i, m, s, j):
                            dst = (ACC2 if i == 2 else ACC[:]) if m == 0 else V[:]
                            B.taken(act, s, ("dense", j, NG - 1))
                            if m > 1:
                                wait(act, acc_[i], 0, m - 1)
                            act.activation(dst, XM[:, m, :], ACT.Square).then_inc(sq_[i].sem, 1)

                        def norm(i):
                            for g, (a, w) in enumerate(GROUPS):
                                src = SB.read(act, 0, ("sum", i, g))
                                SB.release(act.activation(GR[:, a:a + w], src[:, 0:w], ACT.Ln, scale=1.0 / D, bias=eps[:]),
                                           ("sum", i, g))
                            for g, (a, w) in enumerate(GROUPS):
                                SB.taken(act, 0, ("sum", i, g))
                                act.activation(GR[:, a:a + w], GR[:, a:a + w], ACT.Exp, scale=-0.5).then_inc(rms.sem, 1)

                        for q in range(NQ):
                            src = SB.read(act, 0, ("co", q))
                            SB.release(act.activation(crows[:, 512 * q:512 * q + 512], src[0:27, :], ACT.Copy), ("co", q))
                        gate(0, False)
                        with act.Fori(1, S_OUT) as s:
                            gate(s)
                        for m in range(KT):
                            square(0, m, S_OUT + m // 2, m % 2)
                        norm(0)

                        def relu_squared(f):
                            for m in range(KT):
                                for g, (a, w) in enumerate(GROUPS):
                                    s = f * (2 * HALF) + (S_FFN + m // 2)
                                    B.taken(act, s, ("dense", m % 2, g))
                                    if m:
                                        wait(act, ulo, f, (m - 1) * NG + g + 1)
                                    act.activation(ACC[:, a:a + w], V[:, a:a + w], ACT.Square).then_inc(rsq.sem, 1)

                        with act.Fori(0, NBLK) as f:
                            relu_squared(f)
                        for m in range(KT):
                            square(1, m, S_LAST + HALF + m // 2, m % 2)
                        norm(1)
                        for m in range(KT):
                            s = S_PLE + m
                            for g, (a, w) in enumerate(GROUPS):
                                B.taken(act, s, ("dense", 0, g))
                                if m:
                                    wait(act, upd, m - 1, g + 1)
                                act.activation(SG[:, a:a + w], V2[:, a:a + w], ACT.Tanh, scale=0.5).then_inc(gsig.sem, 1)
                            wait(act, upd, m, NG)
                            dst = ACC2 if m == 0 else V[:]
                            if m > 1:
                                wait(act, acc_[2], 0, m - 1)
                            act.activation(dst, XM[:, m, :], ACT.Square).then_inc(sq_[2].sem, 1)
                        src = SB.read(act, 0, ("token", 2))
                        for i, (n, cols) in enumerate(((P, slice(0, NC)), (NB * NS, slice(NC, NCH)))):
                            act.activation(RT[0:n, cols], src[0:n, cols], ACT.Ln, scale=1.0 / D, bias=eps[0:n, :]).then_inc(rt.sem, 1)
                        for i, (n, cols) in enumerate(((P, slice(0, NC)), (NB * NS, slice(NC, NCH)))):
                            wait(act, rt, 0, i + 1)
                            act.activation(RT[0:n, cols], RT[0:n, cols], ACT.Exp, scale=-0.5).then_inc(rt.sem, 1)
                        wait(act, rt, 0, 4)
                        for c in range(NCH):
                            w = L if c < NC else NB * NS
                            slot = dense[2 * (c % 3)]
                            src = B.read(act, S_END + c // 3, slot)
                            B.release(act.activation(yrow(c)[0:w, 0:512], src[0:w, :], ACT.Copy, scale=RT[0:w, c:c + 1]), slot)

                    @block.vector
                    def _(dve):
                        def branch(i):
                            for k in range(KT):
                                if k % 2 == 0:
                                    wait(dve, s_br[k // 2], i, 1)
                                dve.tensor_copy(NHI[:, k, :], rraw[:, k, :]).then_inc(bhi.sem, 1)
                                if k % 2:
                                    wait(dve, bhi, i, k + 1)
                                    dve.tensor_tensor(NLO[:, k, :], rraw[:, k, :], NHI[:, k, :], ALU.subtract).then_inc(blod.sem, 1)

                        def mix_first(s):
                            for g, (a, w) in enumerate(GROUPS):
                                B.taken(dve, s, ("dense", 0, g))
                                src = B.read(dve, s, ("dense", 1, g))
                                B.release(dve.scalar_tensor_tensor(XM[:, bass.ds(s, 1), a:a + w], GR[:, a:a + w].unsqueeze(1), 1.0,
                                                                   src[:, 0:w].unsqueeze(1), ALU.add, ALU.mult), ("dense", 1, g))

                        def mix_second(i):
                            s = i + S_B
                            for g, (a, w) in enumerate(GROUPS):
                                B.taken(dve, s, ("dense", 0, g))
                                src = B.read(dve, s, ("dense", 1, g))
                                dve.scalar_tensor_tensor(GR[:, a:a + w], GR[:, a:a + w], 1.0, src[:, 0:w], ALU.add,
                                                         ALU.mult).then_inc(mixed.sem, 1)
                                wait(dve, mixed, i, g + 1)
                                x = XM[:, bass.ds(i, 1), a:a + w]
                                B.release(dve.tensor_tensor(x, x, GR[:, a:a + w].unsqueeze(1), ALU.add), ("dense", 1, g))

                        def mix_split(k):
                            dve.tensor_copy(UHI[:, k, :], XM[:, k, :]).then_inc(mhi.sem, 1)
                            if k % 2:
                                wait(dve, mhi, 0, k + 1)
                                dve.tensor_tensor(ULO[:, k, :], XM[:, k, :], UHI[:, k, :], ALU.subtract).then_inc(mlo.sem, 1)

                        def mix_last():
                            s, k = S_OUT - 1, KT - 1
                            for g, (a, w) in enumerate(GROUPS):
                                B.taken(dve, s, ("dense", 0, g))
                                src = B.read(dve, s, ("dense", 1, g))
                                dve.scalar_tensor_tensor(GR[:, a:a + w], GR[:, a:a + w], 1.0, src[:, 0:w], ALU.add,
                                                         ALU.mult).then_inc(mixed.sem, 1)
                                wait(dve, mixed, k, g + 1)
                                x = XM[:, k, a:a + w]
                                B.release(dve.tensor_tensor(x, x, GR[:, a:a + w], ALU.add), ("dense", 1, g))
                                B.taken(dve, s, ("dense", 1, g))
                                dve.tensor_copy(UHI[:, k, a:a + w], x).then_inc(mhi.sem, 1)
                                wait(dve, mhi, 0, KT + g)
                                dve.tensor_tensor(ULO[:, k, a:a + w], x, UHI[:, k, a:a + w], ALU.subtract).then_inc(mlo.sem, 1)

                        def x_add(s, j, m):
                            for g, (a, w) in enumerate(GROUPS):
                                src = B.read(dve, s, ("dense", j, g))
                                B.release(dve.tensor_tensor(XM[:, m, a:a + w], XM[:, m, a:a + w], src[:, 0:w], ALU.add),
                                          ("dense", j, g))

                        def n_split(i, m, s, j):
                            g_ = (gf, gp)[i]
                            B.taken(dve, s, ("dense", j, NG - 1))
                            dve.tensor_scalar(NHI[:, m, :], XM[:, m, :], g_[:, m:m + 1], None, ALU.mult).then_inc(nhi_[i].sem, 1)
                            wait(dve, nhi_[i], 0, m + 1)
                            dve.scalar_tensor_tensor(NLO[:, m, :], XM[:, m, :], g_[:, m:m + 1], NHI[:, m, :], ALU.mult,
                                                     ALU.subtract).then_inc(nlo_[i].sem, 1)

                        def relu(f, m, lead):
                            s = f * (2 * HALF) + (S_FFN + m // 2)
                            j = m % 2
                            for g, (a, w) in enumerate(GROUPS):
                                if lead and m == 0:
                                    wait(dve, rms, 0, g + 1)
                                if m:
                                    wait(dve, rsq, f, (m - 1) * NG + g + 1)
                                src = B.read(dve, s, ("dense", j, g))
                                B.release(dve.scalar_tensor_tensor(V[:, a:a + w], src[:, 0:w], 0.0, GR[:, a:a + w], ALU.max,
                                                                   ALU.mult), ("dense", j, g))
                            for g, (a, w) in enumerate(GROUPS):
                                n = m * NG + g + 1
                                wait(dve, rsq, f, n)
                                dve.tensor_copy(UHI[:, m, a:a + w], ACC[:, a:a + w]).then_inc(uhi.sem, 1)
                                wait(dve, uhi, f, n)
                                dve.tensor_tensor(ULO[:, m, a:a + w], ACC[:, a:a + w], UHI[:, m, a:a + w],
                                                  ALU.subtract).then_inc(ulo.sem, 1)

                        def block_(f, lead=False, last=False):
                            s = f * (2 * HALF) + S_FFN
                            for m in range(KT):
                                WS.split_hi(dve, s + m // 2 + m % 2, (m + 1) % 2, B)
                                relu(f, m, lead)
                            for m in range(KT):
                                WS.split_hi(dve, s + HALF + m // 2 + m % 2, (m + 1) % 2, B)
                                x_add(s + HALF + m // 2, m % 2, m)
                                if last:
                                    n_split(1, m, s + HALF + m // 2, m % 2)

                        def gain(m):
                            wait(dve, sq_[2], 0, m + 1)
                            dve.tensor_scalar(XM[:, m, :], XM[:, m, :], gl_[:, m:m + 1], None, ALU.mult).then_inc(y.sem, 1)

                        WS.split_hi(dve, 0, 0, B)
                        WS.split_hi(dve, 0, 1, B)
                        branch(0)
                        WS.split_hi(dve, 1, 0, B)
                        mix_first(0)
                        dve.wait_ge(s_g, 48)
                        wait(dve, s_co, 0, 2)
                        with dve.Fori(1, KT) as s:
                            WS.split_hi(dve, s, 1, B)
                            WS.split_hi(dve, s + 1, 0, B)
                            mix_first(s)
                        branch(1)
                        WS.split_hi(dve, S_B, 1, B)
                        WS.split_hi(dve, S_B + 1, 0, B)
                        mix_second(0)
                        with dve.Fori(1, KT - 1) as i:
                            WS.split_hi(dve, i + S_B, 1, B)
                            WS.split_hi(dve, i + (S_B + 1), 0, B)
                            mix_second(i)
                        WS.split_hi(dve, S_OUT - 1, 1, B)
                        WS.split_hi(dve, S_OUT, 0, B)
                        B.taken(dve, S_OUT - 2, ("dense", 1, NG - 1))
                        for k in range(KT - 1):
                            mix_split(k)
                        mix_last()
                        for m in range(KT):
                            s, j = S_OUT + m // 2, m % 2
                            WS.split_hi(dve, s + j, 1 - j, B)
                            if m == 0 or m == KT - 1:
                                wait(dve, s_x[m // (KT - 1)], 0, 1)
                            x_add(s, j, m)
                            n_split(0, m, s, j)
                        block_(0, lead=True)
                        with dve.Fori(1, NBLK - 1) as f:
                            block_(f)
                        block_(NBLK - 1, last=True)
                        for m in range(KT):
                            s = S_PLE + m
                            WS.split_hi(dve, s, 1, B, kt=PLE // P)
                            for g, (a, w) in enumerate(GROUPS):
                                if m == 0:
                                    wait(dve, rms, 1, g + 1)
                                else:
                                    wait(dve, gsig, m - 1, g + 1)
                                src = B.read(dve, s, ("dense", 0, g))
                                B.release(dve.tensor_tensor(V2[:, a:a + w], src[:, 0:w], GR[:, a:a + w], ALU.mult), ("dense", 0, g))
                            if m == 0:
                                for t in range(6):
                                    e, q = t % 2, t // 2
                                    a, w = GROUPS[q]
                                    src = SB.read(dve, 0, ("p", t))
                                    dve.tensor_copy(PHI[:, e, a:a + w], src[:, 0:w]).then_inc(phi.sem, 1)
                                    wait(dve, phi, 0, t + 1)
                                    SB.release(dve.tensor_tensor(PLO[:, e, a:a + w], src[:, 0:w], PHI[:, e, a:a + w],
                                                                 ALU.subtract), ("p", t))
                            if m < KT - 1:
                                WS.split_hi(dve, s + 1, 0, B)
                            for g, (a, w) in enumerate(GROUPS):
                                wait(dve, gsig, m, g + 1)
                                src = B.read(dve, s, ("dense", 1, g))
                                B.release(dve.scalar_tensor_tensor(SG[:, a:a + w], SG[:, a:a + w], 1.0, src[:, 0:w], ALU.add,
                                                                   ALU.mult), ("dense", 1, g))
                                B.taken(dve, s, ("dense", 1, g))
                                dve.scalar_tensor_tensor(XM[:, m, a:a + w], SG[:, a:a + w], 0.5, XM[:, m, a:a + w], ALU.mult,
                                                         ALU.add).then_inc(upd.sem, 1)
                            if m:
                                gain(m - 1)
                        gain(KT - 1)
                        wait(dve, rt, 0, 4)
                        for c in range(NCH):
                            n = L if c < NC else NB * NS
                            slot = dense[2 * (c % 3) + 1]
                            src = B.read(dve, S_END + c // 3, slot)
                            B.release(dve.tensor_scalar(yrow(c)[0:n, 512:D], src[0:n, :], RT[0:n, c:c + 1], None, ALU.mult), slot)

        stage(prologue)
        stage(gates)
        stage(delta)
        stage(mlstm)
        gts.close()
        stage(tail)


_INS = ["x_prompt", "x_sample", "p_prompt", "p_sample", "state_mlstm_C", "state_mlstm_n", "state_mlstm_m",
        "state_gdn_S", "state_gdn_conv", "g_mix", "w_in", "b_igate", "b_fgate", "g_norm_a", "conv_w", "a_log",
        "dt_bias", "g_norm_b", "w_pa", "w_pb", "w_out", "g_ffn", "w_up", "w_down", "g_ple", "w_pg", "w_pp",
        "g_final"]
_OUTS = [(1, SEQ, D), (NB, NS, D),
         (1, 1, H_A, DK, DV_A), (1, 1, H_A, DK), (1, 1, H_A), (1, 1, H_B, DK, DV_B), (1, 1, HALO, 3 * H_B * P),
         (1, NB, H_A, DK, DV_A), (1, NB, H_A, DK), (1, NB, H_A), (1, NB, H_B, DK, DV_B), (1, NB, HALO, 3 * H_B * P)]


def kernel(**inputs):
    import numpy as _np
    import concourse.bacc as _bacc
    from concourse import mybir as _mybir
    from concourse.bass_utils import run_bass_kernel_spmd as _run

    nc = _bacc.Bacc("TRN2", target_bir_lowering=False, num_devices=1)
    arrays, args = {}, []
    for name in _INS:
        a = _np.ascontiguousarray(inputs[name])
        arrays[f"in_{name}_dram"] = a
        args.append(nc.dram_tensor(f"in_{name}_dram", a.shape, _mybir.dt.from_np(a.dtype), kind="ExternalInput").ap())
    for i, shape in enumerate(_OUTS):
        dt = _mybir.dt.from_np(_np.dtype("float32"))
        args.append(nc.dram_tensor(f"out_{i}_dram", shape, dt, kind="ExternalOutput").ap())
    build(nc, *args)
    r = _run(nc, [arrays], core_ids=[0])
    return tuple(r.results[0][f"out_{i}_dram"] for i in range(len(_OUTS)))
```
